# Optimizing a Trainium2 kernel written in Bass

```python
import math
import jax
import jax.numpy as jnp
from jax import lax
import numpy as np

D_MODEL = 1024
BATCH = 1
SEQ = 512
DEPTH = 2

CTX_LEN = 256
GRID_W = 64

N_BRANCH = 4
BRANCH_W = D_MODEL // N_BRANCH

MLA_HEADS = 4
MLA_NOPE = 64
MLA_ROPE = 32
MLA_V = 64
MLA_Q_LORA = 256
MLA_KV_LORA = 128
ML_HEADS = 4
ML_DH = 64
ML_CONV = 3
ML_CHUNK = 64
GLA_HEADS = 4
GLA_DK = 32
GLA_DV = 64
GLA_RANK = 16
GLA_TAU = 16.0
GLA_CHUNK = 64
DIFF_HEADS = 4
DIFF_DQK = 32
DIFF_DV = 64
ROPE_DIM = 32
ROPE_BASE = 10000.0
Q_BLOCK = 128
N_EXPERTS = 16
EC_CAPACITY = 2
EXPERT_FF = 1408

NEG_BIG = -1e30
EPS = 1e-6

MLA_COLS = (MLA_Q_LORA, MLA_KV_LORA, MLA_ROPE)
ML_COLS = (2 * ML_HEADS * ML_DH, ML_HEADS * ML_DH, ML_HEADS * ML_DH, 2 * ML_HEADS, 2 * ML_HEADS)
GLA_COLS = (GLA_HEADS * GLA_DK, GLA_HEADS * GLA_DK, GLA_HEADS * GLA_DV, GLA_HEADS * GLA_DV, 2 * GLA_RANK)
DIFF_COLS = (DIFF_HEADS * 2 * DIFF_DQK, DIFF_HEADS * 2 * DIFF_DQK, DIFF_HEADS * DIFF_DV)
MIXER_COLS = (sum(MLA_COLS), sum(ML_COLS), sum(GLA_COLS), sum(DIFF_COLS))
N_IN = sum(MIXER_COLS)

kernel_name = 'hybrid_mla_mlstm_gla_diffattn_ecmoe_block'

def _split(z, sizes):
    return jnp.split(z, np.cumsum(sizes)[:-1].tolist(), axis=-1)

def _chunk(a, size):
    return a.reshape((a.shape[0], a.shape[1] // size, size) + a.shape[2:])

def _flip(a, direction):
    return a if (a is None or direction == 0) else jnp.flip(a, axis=1)

def rms_norm(x, g):
    xf = x.astype(jnp.float32)
    y = xf * lax.rsqrt(jnp.mean(xf * xf, axis=-1, keepdims=True) + EPS)
    return (y * g.astype(jnp.float32)).astype(x.dtype)

def head_rms(x, g, n_heads):
    shp = x.shape
    xh = x.reshape(shp[:-1] + (n_heads, shp[-1] // n_heads))
    return rms_norm(xh, g.reshape(n_heads, -1)).reshape(shp)

def modulate(x, g, shift, scale):
    return rms_norm(x, g) * (1 + scale[:, None]) + shift[:, None]

def axial_rope_tables(rows):
    nf = ROPE_DIM // 4
    row = jnp.repeat(jnp.arange(rows), GRID_W)
    col = jnp.tile(jnp.arange(GRID_W), rows)
    inv_freq = ROPE_BASE ** (-jnp.arange(nf, dtype=jnp.float32) / nf)
    ang = jnp.stack([row, col], axis=-1).astype(jnp.float32)[..., None] * inv_freq
    return jnp.cos(ang), jnp.sin(ang)

def apply_rope(x, rope):
    cos, sin = rope
    nf = ROPE_DIM // 4
    shp = x.shape
    xr = x.astype(jnp.float32).reshape(shp[:-1] + (2, 2, nf))
    x1, x2 = xr[..., 0, :], xr[..., 1, :]
    bshape = cos.shape[:1] + (1,) * (x.ndim - 3) + cos.shape[1:]
    cb, sb = cos.reshape(bshape), sin.reshape(bshape)
    out = jnp.stack([x1 * cb - x2 * sb, x2 * cb + x1 * sb], axis=-2)
    return out.reshape(shp).astype(x.dtype)

def sweep_query_blocks(q, block_fn):
    b, t = q.shape[0], q.shape[1]
    qb = q.reshape((b, t // Q_BLOCK, Q_BLOCK) + q.shape[2:]).swapaxes(0, 1)
    out = lax.map(block_fn, qb).swapaxes(0, 1)
    return out.reshape((b, t) + out.shape[3:])

def mla_attention(q, k, v):
    scale = (MLA_NOPE + MLA_ROPE) ** -0.5

    def blk(qb):
        s = jnp.einsum('bqhd,bkhd->bhqk', qb, k).astype(jnp.float32) * scale
        p = jax.nn.softmax(s, axis=-1).astype(v.dtype)
        return jnp.einsum('bhqk,bkhd->bqhd', p, v)

    return sweep_query_blocks(q, blk)

def diff_attention(q, k, v, lam):
    scale = DIFF_DQK ** -0.5

    def blk(qb):
        s = jnp.einsum('bqhmd,bkhmd->bhmqk', qb, k).astype(jnp.float32) * scale
        p = jax.nn.softmax(s, axis=-1)
        a = (p[:, :, 0] - lam * p[:, :, 1]).astype(v.dtype)
        return jnp.einsum('bhqk,bkhd->bqhd', a, v)

    return sweep_query_blocks(q, blk)

def short_conv(x, w, b):
    pad = ML_CONV // 2
    t = x.shape[1]
    xp = jnp.pad(x, ((0, 0), (pad, pad), (0, 0)))
    return sum(xp[:, j:j + t] * w[j] for j in range(ML_CONV)) + b

def mlstm_dir(q, k, v, ig, lf, init, want_out):
    kc, vc, igc, lfc = (_chunk(a, ML_CHUNK) for a in (k, v, ig, lf))
    bcum = jnp.cumsum(lfc, axis=2)
    b_end = bcum[:, :, -1]
    w_log = b_end[:, :, None] - bcum + igc
    m_loc = jnp.max(w_log, axis=2)
    w = jnp.exp(w_log - m_loc[:, :, None])
    c_loc = jnp.einsum('bclh,bclhv,bclhk->bchvk', w, vc, kc)
    n_loc = jnp.einsum('bclh,bclhk->bchk', w, kc)

    def step(carry, inp):
        c_st, n_st, m_st = carry
        be, ml, cl, nl = inp
        m_new = jnp.maximum(be + m_st, ml)
        a = jnp.exp(be + m_st - m_new)
        g = jnp.exp(ml - m_new)
        c_new = a[..., None, None] * c_st + g[..., None, None] * cl
        n_new = a[..., None] * n_st + g[..., None] * nl
        return (c_new, n_new, m_new), (c_st, n_st, m_st)

    xs = tuple(jnp.moveaxis(a, 1, 0) for a in (b_end, m_loc, c_loc, n_loc))
    final, starts = lax.scan(step, init, xs)
    if not want_out:
        return None, final
    c0, n0, m0 = (jnp.moveaxis(a, 0, 1) for a in starts)
    qc = _chunk(q, ML_CHUNK)
    causal = jnp.tril(jnp.ones((ML_CHUNK, ML_CHUNK), dtype=bool))
    bt = jnp.swapaxes(bcum, 2, 3)
    it = jnp.swapaxes(igc, 2, 3)
    d_log = jnp.where(causal, bt[..., :, None] - bt[..., None, :] + it[..., None, :], -jnp.inf)
    inter = bt + m0[..., None]
    m_t = jnp.maximum(inter, jnp.max(d_log, axis=-1))
    s = jnp.exp(d_log - m_t[..., None]) * jnp.einsum('bclhd,bcshd->bchls', qc, kc)
    a_int = jnp.exp(inter - m_t)
    num = jnp.einsum('bchls,bcshv->bclhv', s, vc) + jnp.einsum('bchl,bclhk,bchvk->bclhv', a_int, qc, c0)
    den = jnp.sum(s, axis=-1) + a_int * jnp.einsum('bclhk,bchk->bchl', qc, n0)
    h = num / jnp.swapaxes(jnp.maximum(jnp.abs(den), jnp.exp(-m_t)), 2, 3)[..., None]
    return h.reshape(v.shape), final

def gla_dir(q, k, v, lg, init, want_out):
    kc, vc, gc = (_chunk(a, GLA_CHUNK) for a in (k, v, lg))
    gcum = jnp.cumsum(gc, axis=2)
    g_end = gcum[:, :, -1]
    s_loc = jnp.einsum('bclhk,bclhv->bchkv', kc * jnp.exp(g_end[:, :, None] - gcum), vc)

    def step(s_st, inp):
        ge, sl = inp
        return jnp.exp(ge)[..., None] * s_st + sl, s_st

    final, starts = lax.scan(step, init, (jnp.moveaxis(g_end, 1, 0), jnp.moveaxis(s_loc, 1, 0)))
    if not want_out:
        return None, final
    s0 = jnp.moveaxis(starts, 0, 1)
    causal = jnp.tril(jnp.ones((GLA_CHUNK, GLA_CHUNK), dtype=bool))
    q_dec = _chunk(q, GLA_CHUNK) * jnp.exp(gcum)
    att = jnp.einsum('bclhk,bcshk->bchls', q_dec, kc * jnp.exp(-gcum))
    att = jnp.where(causal, att, 0.0)
    o = jnp.einsum('bchls,bcshv->bclhv', att, vc) + jnp.einsum('bclhk,bchkv->bclhv', q_dec, s0)
    return o.reshape(v.shape), final

def run_bidirectional(dir_fn, ctx_inputs, lat_inputs, init, need_ctx):
    out_c, out_l = None, None
    for d in range(2):
        h_c, fin_c = dir_fn(*[_flip(a, d) for a in ctx_inputs[d]], init, need_ctx)
        h_l, _ = dir_fn(*[_flip(a, d) for a in lat_inputs[d]], fin_c, True)
        h_l = _flip(h_l, d)
        out_l = h_l if out_l is None else out_l + h_l
        if need_ctx:
            h_c = _flip(h_c, d)
            out_c = h_c if out_c is None else out_c + h_c
    return out_c, out_l

def mla_branch(zc, zl, rope, g_q_lat, w_uq, g_kv_lat, w_ukv, need_ctx):
    def queries(z, rot):
        q_lat = _split(z, MLA_COLS)[0]
        q = (rms_norm(q_lat, g_q_lat) @ w_uq).reshape(z.shape[:2] + (MLA_HEADS, MLA_NOPE + MLA_ROPE))
        q_nope, q_rope = q[..., :MLA_NOPE], q[..., MLA_NOPE:]
        if rot is not None:
            q_rope = apply_rope(q_rope, rot)
        return jnp.concatenate([q_nope, q_rope], axis=-1)

    def keys_values(z, rot):
        _, kv_lat, k_rope = _split(z, MLA_COLS)
        kv = (rms_norm(kv_lat, g_kv_lat) @ w_ukv).reshape(z.shape[:2] + (MLA_HEADS, MLA_NOPE + MLA_V))
        k_nope, v = kv[..., :MLA_NOPE], kv[..., MLA_NOPE:]
        k_rope = k_rope[:, :, None, :]
        if rot is not None:
            k_rope = apply_rope(k_rope, rot)
        k = jnp.concatenate([k_nope, jnp.broadcast_to(k_rope, k_nope.shape[:-1] + (MLA_ROPE,))], axis=-1)
        return k, v

    def flat(y):
        return y.reshape(y.shape[:2] + (MLA_HEADS * MLA_V,))

    k_c, v_c = keys_values(zc, None)
    k_l, v_l = keys_values(zl, rope)
    y_l = mla_attention(queries(zl, rope), jnp.concatenate([k_c, k_l], axis=1), jnp.concatenate([v_c, v_l], axis=1))
    y_c = flat(mla_attention(queries(zc, None), k_c, v_c)) if need_ctx else None
    return y_c, flat(y_l)

def mlstm_branch(zc, zl, w_conv, b_conv, b_igate, b_fgate, g_out, need_ctx):
    def prep(z):
        bsz, t = z.shape[:2]
        hd = (bsz, t, ML_HEADS, ML_DH)
        qk, v, o, ig, fg = _split(z, ML_COLS)
        qk = jax.nn.silu(short_conv(qk, w_conv, b_conv)).astype(jnp.float32)
        q = qk[..., :ML_HEADS * ML_DH].reshape(hd)
        k = qk[..., ML_HEADS * ML_DH:].reshape(hd) * ML_DH ** -0.5
        v = v.astype(jnp.float32).reshape(hd)
        ig = ig.astype(jnp.float32).reshape(bsz, t, 2, ML_HEADS) + b_igate
        lf = jax.nn.log_sigmoid(fg.astype(jnp.float32).reshape(bsz, t, 2, ML_HEADS) + b_fgate)
        return q, k, v, o, ig, lf

    q_c, k_c, v_c, o_c, ig_c, lf_c = prep(zc)
    q_l, k_l, v_l, o_l, ig_l, lf_l = prep(zl)
    bsz = zl.shape[0]
    init = (jnp.zeros((bsz, ML_HEADS, ML_DH, ML_DH), jnp.float32),
            jnp.zeros((bsz, ML_HEADS, ML_DH), jnp.float32),
            jnp.full((bsz, ML_HEADS), NEG_BIG, jnp.float32))
    ctx_in = [(q_c if need_ctx else None, k_c, v_c, ig_c[:, :, d], lf_c[:, :, d]) for d in range(2)]
    lat_in = [(q_l, k_l, v_l, ig_l[:, :, d], lf_l[:, :, d]) for d in range(2)]
    h_c, h_l = run_bidirectional(mlstm_dir, ctx_in, lat_in, init, need_ctx)

    def finish(h, o):
        return jax.nn.sigmoid(o) * head_rms(h.reshape(o.shape).astype(o.dtype), g_out, ML_HEADS)

    return (finish(h_c, o_c) if need_ctx else None), finish(h_l, o_l)

def gla_branch(zc, zl, w_alpha2, b_alpha, g_out, need_ctx):
    def prep(z):
        bsz, t = z.shape[:2]
        q, k, v, r, a = _split(z, GLA_COLS)
        q = q.astype(jnp.float32).reshape(bsz, t, GLA_HEADS, GLA_DK) * GLA_DK ** -0.5
        k = k.astype(jnp.float32).reshape(bsz, t, GLA_HEADS, GLA_DK)
        v = v.astype(jnp.float32).reshape(bsz, t, GLA_HEADS, GLA_DV)
        zg = jnp.einsum('btnr,nrk->btnk', a.reshape(bsz, t, 2, GLA_RANK), w_alpha2) + b_alpha
        lg = (jax.nn.log_sigmoid(zg.astype(jnp.float32)) / GLA_TAU).reshape(bsz, t, 2, GLA_HEADS, GLA_DK)
        return q, k, v, r, lg

    q_c, k_c, v_c, r_c, lg_c = prep(zc)
    q_l, k_l, v_l, r_l, lg_l = prep(zl)
    init = jnp.zeros((zl.shape[0], GLA_HEADS, GLA_DK, GLA_DV), jnp.float32)
    ctx_in = [(q_c if need_ctx else None, k_c, v_c, lg_c[:, :, d]) for d in range(2)]
    lat_in = [(q_l, k_l, v_l, lg_l[:, :, d]) for d in range(2)]
    o_c, o_l = run_bidirectional(gla_dir, ctx_in, lat_in, init, need_ctx)

    def finish(o, r):
        return jax.nn.silu(r) * head_rms(o.reshape(r.shape).astype(r.dtype), g_out, GLA_HEADS)

    return (finish(o_c, r_c) if need_ctx else None), finish(o_l, r_l)

def diff_branch(zc, zl, rope, diff_lambda, g_out, lam_init, need_ctx):
    lv = diff_lambda.astype(jnp.float32)
    lam = jnp.exp(jnp.sum(lv[0] * lv[1])) - jnp.exp(jnp.sum(lv[2] * lv[3])) + lam_init

    def qkv(z, rot):
        bsz, t = z.shape[:2]
        q, k, v = _split(z, DIFF_COLS)
        qk_shape = (bsz, t, DIFF_HEADS, 2, DIFF_DQK)
        q, k = q.reshape(qk_shape), k.reshape(qk_shape)
        if rot is not None:
            q, k = apply_rope(q, rot), apply_rope(k, rot)
        return q, k, v.reshape(bsz, t, DIFF_HEADS, DIFF_DV)

    def finish(o):
        o = o.reshape(o.shape[:2] + (DIFF_HEADS * DIFF_DV,))
        return head_rms(o, g_out, DIFF_HEADS) * (1.0 - lam_init)

    q_c, k_c, v_c = qkv(zc, None)
    q_l, k_l, v_l = qkv(zl, rope)
    y_l = finish(diff_attention(q_l, jnp.concatenate([k_c, k_l], axis=1), jnp.concatenate([v_c, v_l], axis=1), lam))
    y_c = finish(diff_attention(q_c, k_c, v_c, lam)) if need_ctx else None
    return y_c, y_l

def merge_branches(h, ys, w_branch, w_gate, b_gate, w_out):
    y = jnp.stack(ys, axis=2)
    p = jnp.einsum('btnc,ncd->btnd', y, w_branch)
    g = jax.nn.sigmoid(h @ w_gate + b_gate).reshape(p.shape)
    return jnp.sum(g * p, axis=2) @ w_out

def ec_moe(h, w_router, w_e_gate, w_e_up, w_e_down):
    b, t, d = h.shape
    cap = EC_CAPACITY * t // N_EXPERTS
    aff = jax.nn.softmax((h @ w_router).astype(jnp.float32), axis=-1)
    vals, idx = lax.top_k(jnp.swapaxes(aff, 1, 2), cap)
    xs = jax.vmap(lambda hb, ib: hb[ib])(h, idx)
    hid = jax.nn.silu(jnp.einsum('becd,edf->becf', xs, w_e_gate)) * jnp.einsum('becd,edf->becf', xs, w_e_up)
    ys = jnp.einsum('becf,efd->becd', hid, w_e_down) * vals[..., None].astype(h.dtype)
    return jax.vmap(lambda yb, ib: jnp.zeros((t, d), yb.dtype).at[ib.reshape(-1)].add(yb.reshape(-1, d)))(ys, idx)

def hybrid_layer(x_c, x_l, silu_c, silu_cc, rope, layer_idx, need_ctx,
                 w_ada, b_ada, g_mix_pre, g_mix_post, g_ffn_pre, g_ffn_post, w_in,
                 g_q_lat, w_uq, g_kv_lat, w_ukv,
                 w_conv, b_conv, b_igate, b_fgate, g_mlstm_out,
                 w_alpha2, b_alpha, g_gla_out,
                 diff_lambda, g_diff_out,
                 w_branch, w_gate, b_gate, w_out,
                 w_router, w_e_gate, w_e_up, w_e_down):
    lam_init = 0.8 - 0.6 * math.exp(-0.3 * layer_idx)
    mod_l = jnp.split(silu_c @ w_ada + b_ada, 6, axis=-1)
    mod_c = jnp.split(silu_cc @ w_ada + b_ada, 6, axis=-1)

    h_l = modulate(x_l, g_mix_pre, mod_l[0], mod_l[1])
    h_c = modulate(x_c, g_mix_pre, mod_c[0], mod_c[1])
    z_l = _split(h_l @ w_in, MIXER_COLS)
    z_c = _split(h_c @ w_in, MIXER_COLS)
    a_c, a_l = mla_branch(z_c[0], z_l[0], rope, g_q_lat, w_uq, g_kv_lat, w_ukv, need_ctx)
    b_c, b_l = mlstm_branch(z_c[1], z_l[1], w_conv, b_conv, b_igate, b_fgate, g_mlstm_out, need_ctx)
    c_c, c_l = gla_branch(z_c[2], z_l[2], w_alpha2, b_alpha, g_gla_out, need_ctx)
    d_c, d_l = diff_branch(z_c[3], z_l[3], rope, diff_lambda, g_diff_out, lam_init, need_ctx)
    y_l = merge_branches(h_l, (a_l, b_l, c_l, d_l), w_branch, w_gate, b_gate, w_out)
    x_l = x_l + mod_l[2][:, None] * rms_norm(y_l, g_mix_post)

    f_l = ec_moe(modulate(x_l, g_ffn_pre, mod_l[3], mod_l[4]), w_router, w_e_gate, w_e_up, w_e_down)
    x_l = x_l + mod_l[5][:, None] * rms_norm(f_l, g_ffn_post)

    if need_ctx:
        y_c = merge_branches(h_c, (a_c, b_c, c_c, d_c), w_branch, w_gate, b_gate, w_out)
        x_c = x_c + mod_c[2][:, None] * rms_norm(y_c, g_mix_post)
        f_c = ec_moe(modulate(x_c, g_ffn_pre, mod_c[3], mod_c[4]), w_router, w_e_gate, w_e_up, w_e_down)
        x_c = x_c + mod_c[5][:, None] * rms_norm(f_c, g_ffn_post)
    return x_c, x_l

def setup_inputs(seed: int = 0) -> dict:
    key = jax.random.key(seed)
    ks = iter(jax.random.split(key, 40))
    L, D = DEPTH, D_MODEL

    def nrm(shape, scale):
        return jax.random.normal(next(ks), shape, jnp.float32) * scale

    def gain(shape):
        return 1.0 + nrm(shape, 0.02)

    return {
        'x': nrm((BATCH, SEQ, D), 1.0),
        'c': nrm((BATCH, D), 1.0),
        'ctx': nrm((BATCH, CTX_LEN, D), 1.0),
        'c_ctx': nrm((D,), 1.0),
        'w_ada': nrm((L, D, 6 * D), 0.5 * D ** -0.5),
        'b_ada': nrm((L, 6 * D), 0.01),
        'g_mix_pre': gain((L, D)),
        'g_mix_post': gain((L, D)),
        'g_ffn_pre': gain((L, D)),
        'g_ffn_post': gain((L, D)),
        'w_in': nrm((L, D, N_IN), D ** -0.5),
        'g_q_lat': gain((L, MLA_Q_LORA)),
        'w_uq': nrm((L, MLA_Q_LORA, MLA_HEADS * (MLA_NOPE + MLA_ROPE)), MLA_Q_LORA ** -0.5),
        'g_kv_lat': gain((L, MLA_KV_LORA)),
        'w_ukv': nrm((L, MLA_KV_LORA, MLA_HEADS * (MLA_NOPE + MLA_V)), MLA_KV_LORA ** -0.5),
        'w_conv': nrm((L, ML_CONV, 2 * ML_HEADS * ML_DH), ML_CONV ** -0.5),
        'b_conv': nrm((L, 2 * ML_HEADS * ML_DH), 0.01),
        'b_igate': nrm((L, 2, ML_HEADS), 0.1),
        'b_fgate': jnp.linspace(3.0, 6.0, ML_HEADS)[None, None] + nrm((L, 2, ML_HEADS), 0.1),
        'g_mlstm_out': gain((L, ML_HEADS * ML_DH)),
        'w_alpha2': nrm((L, 2, GLA_RANK, GLA_HEADS * GLA_DK), GLA_RANK ** -0.5),
        'b_alpha': nrm((L, 2, GLA_HEADS * GLA_DK), 0.01),
        'g_gla_out': gain((L, GLA_HEADS * GLA_DV)),
        'diff_lambda': nrm((L, 4, DIFF_DQK), 0.1),
        'g_diff_out': gain((L, DIFF_HEADS * DIFF_DV)),
        'w_branch': nrm((L, N_BRANCH, BRANCH_W, D), BRANCH_W ** -0.5),
        'w_gate': nrm((L, D, N_BRANCH * D), D ** -0.5),
        'b_gate': nrm((L, N_BRANCH * D), 0.01),
        'w_out': nrm((L, D, D), D ** -0.5),
        'w_router': nrm((L, D, N_EXPERTS), D ** -0.5),
        'w_e_gate': nrm((L, N_EXPERTS, D, EXPERT_FF), D ** -0.5),
        'w_e_up': nrm((L, N_EXPERTS, D, EXPERT_FF), D ** -0.5),
        'w_e_down': nrm((L, N_EXPERTS, EXPERT_FF, D), EXPERT_FF ** -0.5),
    }

def reference(x, c, ctx, c_ctx, w_ada, b_ada, g_mix_pre, g_mix_post, g_ffn_pre, g_ffn_post, w_in,
              g_q_lat, w_uq, g_kv_lat, w_ukv, w_conv, b_conv, b_igate, b_fgate, g_mlstm_out,
              w_alpha2, b_alpha, g_gla_out, diff_lambda, g_diff_out,
              w_branch, w_gate, b_gate, w_out, w_router, w_e_gate, w_e_up, w_e_down):
    rows = x.shape[1] // GRID_W
    rope = axial_rope_tables(rows)
    silu_c = jax.nn.silu(c)
    silu_cc = jax.nn.silu(c_ctx)[None]
    x_c, x_l = ctx, x
    for i in range(DEPTH):
        x_c, x_l = hybrid_layer(
            x_c, x_l, silu_c, silu_cc, rope, i, i < DEPTH - 1,
            w_ada[i], b_ada[i], g_mix_pre[i], g_mix_post[i], g_ffn_pre[i], g_ffn_post[i], w_in[i],
            g_q_lat[i], w_uq[i], g_kv_lat[i], w_ukv[i],
            w_conv[i], b_conv[i], b_igate[i], b_fgate[i], g_mlstm_out[i],
            w_alpha2[i], b_alpha[i], g_gla_out[i],
            diff_lambda[i], g_diff_out[i],
            w_branch[i], w_gate[i], b_gate[i], w_out[i],
            w_router[i], w_e_gate[i], w_e_up[i], w_e_down[i])
    return x_l


_drawn_inputs = setup_inputs


def setup_inputs(seed=0):
    import zlib

    import numpy as np

    out = dict(_drawn_inputs(seed))
    spreads = {}
    factors = {'g_ffn_post': 2.997,
     'g_q_lat': 2.736,
     'g_kv_lat': 2.901,
     'b_conv': 3.397,
     'b_igate': 37.581,
     'g_mlstm_out': 3.59,
     'b_alpha': 23.326,
     'b_gate': 3.307}
    for name, (base, spread) in spreads.items():
        noise = np.random.default_rng([zlib.crc32(name.encode()), seed]).standard_normal(out[name].shape)
        drawn = base * np.exp(spread * noise) if base else spread * noise
        out[name] = jnp.asarray(drawn.astype(out[name].dtype))
    for name, factor in factors.items():
        out[name] = (out[name] * factor).astype(out[name].dtype)
    return out
```

```python
import math
from contextlib import ExitStack

import numpy as np

import concourse.bass as bass
from concourse import mybir

F32 = mybir.dt.float32
ALU = mybir.AluOpType
AF = mybir.ActivationFunctionType
AX = mybir.AxisListType
P = 128

D = 1024
KD = D // P
CTX, LAT = 256, 512
T = CTX + LAT
NT = T // P
CT = CTX // P
DEPTH = 2
NE = 16
FF = 1408
NF = FF // P
CAP_L, CAP_C = 2 * LAT // NE, 2 * CTX // NE
CAPS = CAP_L + CAP_C
EPS = 1e-6
NEG_BIG = -1e30

SLOTS = 3
SLOT = KD * 512
PIECES_ADA = 12
PIECES_EXP = 9
PIECES_IN, PIECES_MERGE = 7, 8 + 2
NEXT_ADA = lambda L: PIECES_ADA if L + 1 < DEPTH else 0
N_IN = [PIECES_ADA]
for _L in range(DEPTH):
    N_IN.append(N_IN[_L] + PIECES_IN + NEXT_ADA(_L) + PIECES_MERGE + PIECES_EXP * NE)
N_ADA = [0] + [N_IN[_L] + PIECES_IN for _L in range(DEPTH - 1)]
N_MERGE = [N_IN[_L] + PIECES_IN + NEXT_ADA(_L) for _L in range(DEPTH)]
N_EXP = [N_MERGE[_L] + PIECES_MERGE for _L in range(DEPTH)]
W_IN_SPLIT = (456, 512, 512, 304, 512, 512, 256)

_PACK = [("g_mix_pre", 8), ("g_ffn_pre", 8), ("g_mix_post", 8), ("g_ffn_post", 8), ("b_ada", 48),
         ("g_q", 2), ("g_kv", 1), ("w_conv", 12), ("b_conv", 4), ("b_alpha", 2), ("g_ml", 2), ("g_gla", 2),
         ("g_diff", 2), ("b_gate", 32), ("w_router", 128), ("lam", 128), ("b_i", 1), ("b_f", 1),
         ("w_alpha", 256), ("w_uq", 768), ("w_ukv", 512)]
PK = {}
_at = 0
for _n, _w in _PACK:
    PK[_n] = (_at, _w)
    _at += _w
PACK_W = _at

_CONST = [("ident", 128), ("ones", 128), ("m_fwd", 128), ("m_bwd", 128), ("heads", 4), ("cos", 64), ("sin", 64),
          ("iota", 64), ("tokens", NT), ("resets", 768), ("rows", 1024), ("eps", 1)]
CO = {}
_at = 0
for _n, _w in _CONST:
    CO[_n] = (_at, _w)
    _at += _w
CONST_W = _at


def constants():
    c = np.zeros((P, CONST_W), np.float32)

    def put(name, a):
        s, w = CO[name]
        c[:a.shape[0], s:s + w] = a

    put("ident", np.eye(P, dtype=np.float32))
    put("ones", np.ones((P, P), np.float32))
    s, t = np.mgrid[0:P, 0:P]
    same = (s // 64) == (t // 64)
    put("m_fwd", (same & (s <= t)).astype(np.float32))
    put("m_bwd", (same & (s >= t)).astype(np.float32))
    put("heads", (np.arange(P)[:, None] // 32 == np.arange(4)[None]).astype(np.float32))
    tok = np.arange(LAT)
    pos = np.stack([tok // 64, tok % 64], -1).astype(np.float32)
    inv = (10000.0 ** (-np.arange(8, dtype=np.float32) / 8)).astype(np.float32)
    ang = (pos[..., None] * inv).astype(np.float32).reshape(4, P, 16)
    put("cos", np.cos(ang).transpose(1, 0, 2).reshape(P, 64))
    put("sin", np.sin(ang).transpose(1, 0, 2).reshape(P, 64))
    put("iota", np.broadcast_to(np.arange(1, 65, dtype=np.float32), (P, 64)))
    put("tokens", (np.arange(NT)[None] * P + np.arange(P)[:, None]).astype(np.float32))
    put("resets", np.broadcast_to((np.arange(T) % 64 != 0).astype(np.float32), (P, T)))
    rows = np.zeros((8, 8, P), np.float32)
    rows[np.arange(8), np.arange(8)] = 1
    put("rows", rows.reshape(8, 1024))
    put("eps", np.full((P, 1), EPS, np.float32))
    return c


class Order:

    def __init__(self, eng, sems, own):
        self.eng, self.sems, self.own = eng, sems, own
        self.n, self.k, self.per, self.e = {}, {}, {}, None

    def value(self, name, add):
        if self.e is None:
            self.n[name] = self.n.get(name, 0) + add
            return self.n[name]
        self.k[name] = self.k.get(name, 0) + add
        return self.e * self.per[name] + (self.n.get(name, 0) + self.k[name])

    def seq(self, ins):
        ins.then_inc(self.sems[self.own], 1)
        self.eng.wait_ge(self.sems[self.own], self.value(self.own, 1))

    def nth(self, name, by=1):
        return self.value(name, by)

    def begin(self, e, per):
        self.e, self.per, self.k = e, per, {}

    def finish_loop(self, iterations):
        assert self.k == self.per, (self.own, self.k, self.per)
        for name, k in self.per.items():
            self.n[name] = self.n.get(name, 0) + iterations * k


def hybrid_layers(nc, I, out, stop=None):
    ctx = ExitStack()
    with ctx:
        def sb(name, cols):
            return ctx.enter_context(nc.sbuf_tensor(name, [P, cols], F32))

        X = sb("X", NT * D)[:, :].rearrange("p (t d) -> p t d", t=NT)
        HT = sb("HT", KD * T)[:, :].rearrange("p (k t) -> p k t", k=KD)
        YTr = sb("YT", 8 * T)[:, :]
        ring = sb("ring", SLOTS * SLOT)
        const = sb("const", CONST_W)
        packs = sb("pack", PACK_W)
        small = sb("small", 660)
        WORK_W = 16896
        work = sb("work", WORK_W)
        YT = YTr.rearrange("p (b i t) -> p b i t", b=4, i=2)
        idx = ctx.enter_context(nc.sbuf_tensor("idx", [P, 2], mybir.dt.uint32))
        first_row = [CTX if L == DEPTH - 1 else 0 for L in range(DEPTH)]
        xn_rows = [nc.dram_tensor(f"xn_rows{L}", (T - first_row[L], D), F32, kind="Internal").ap() for L in range(DEPTH)]
        f_rows = [nc.dram_tensor(f"f_rows{L}", (T - first_row[L], D), F32, kind="Internal").ap() for L in range(DEPTH)]
        banks = [ctx.enter_context(nc.psum_tensor(f"bank{i}", [P, 512], F32)) for i in range(8)]

        def cc(name):
            s, w = CO[name]
            return const[:, s:s + w]

        def pk(name):
            s, w = PK[name]
            return packs[:, s:s + w]

        ident, ones = cc("ident"), cc("ones")

        names = ["dve_order", "act_order", "pool_order", "a_done", "a_free", "d_done", "d_free", "x_free", "row_free", "pv_done",
                 "const_in", "pack_in", "x_in", "w_in0", "w_in1", "w_in2", "out_done", "layer_done",
                 "silc", "mod", "mrow", "ssq", "ms", "rt", "xn", "mla_lat", "mla_sq", "mla_r", "mla_n", "mla_tm", "mla_rope",
                 "att_max", "att_p", "att_a", "hs_ms", "hs_rt", "branch_done", "y_ready", "ml_raw", "ml_conv", "ml_qk", "ml_x",
                 "ml_l", "ml_m", "ml_e", "ml_rows", "ml_w", "ml_mask", "ml_s", "gl_in", "gl_x", "gl_l", "gl_g", "gl_e",
                 "gl_ops", "gl_att", "gl_state", "lam_p", "lam_e", "gate", "mg_prod", "mg_sum", "yo", "diag", "grow",
                 "rt_max", "rt_exp", "aff", "pos", "sel", "chosen", "idx_next", "idx_now", "xn_stored", "zeros", "zeroed",
                 "rows_in", "rows_t", "xs", "gu", "silu", "hid", "hid_t", "hid_f", "ys", "ys_a", "ys_d", "scat", "f_back"]
        sems = {n: ctx.enter_context(nc.semaphore(n)) for n in names}

        def ada_pieces(L):
            return [(512, KD, I["w_ada"][L, :, 512 * p:512 * (p + 1)].rearrange("(k p) n -> p k n", p=P)) for p in range(PIECES_ADA)]

        def in_pieces(L):
            out_, s = [], 0
            for w in W_IN_SPLIT:
                out_.append((w, KD, I["w_in"][L, :, s:s + w].rearrange("(k p) n -> p k n", p=P)))
                s += w
            return out_

        def merge_pieces(L):
            out_ = []
            for half in range(2):
                for n in range(4):
                    c0 = n * D + half * 512
                    out_.append((512, KD, I["w_gate"][L, :, c0:c0 + 512].rearrange("(k p) n -> p k n", p=P)))
            for half in range(2):
                out_.append((512, KD, I["w_out"][L, :, 512 * half:512 * half + 512].rearrange("(k p) n -> p k n", p=P)))
            return out_

        EXP_W = (512, 512, 512, 512, 384, 384)
        EXP_DOWN = (4, 4, 3)

        def slot(n, w=512, k=KD):
            s = (n % SLOTS) * SLOT
            return ring[:, s:s + k * w].rearrange("p (k n) -> p k n", k=k)

        w_in = [sems[f"w_in{i}"] for i in range(SLOTS)]

        def landings(n):
            return 16 * (n // SLOTS + 1)

        marks = {}
        rings = {"a": [(0, (0, 1, 2))], "d": [(0, (3, 4, 5))]}

        def ring_bank(kind, n):
            start, of = [r for r in rings[kind] if r[0] <= n][-1]
            return banks[of[(n - start) % len(of)]]

        def segs(L, queries=False):
            return [(CTX, LAT)] if (L == DEPTH - 1 and queries) else [(CTX, LAT), (0, CTX)]

        def qtiles(L):
            return list(range(CT if L == DEPTH - 1 else 0, NT))

        def area(start, cols):
            assert start + cols <= WORK_W, (start, cols)
            return work[:, start:start + cols]

        def views(spec):
            at, d = 0, {}
            for n, w in spec:
                d[n] = area(at, w)
                at += w
            return d

        V_N = views([("xn", NT * D), ("junk", D)])
        a_qT = area(0, 4 * T).rearrange("p (h t) -> p h t", h=4)
        a_kT = area(4 * T, 4 * T).rearrange("p (h t) -> p h t", h=4)
        a_ql = area(0, 2 * T).rearrange("p (i t) -> p i t", i=2)
        a_kv = area(2 * T, T)
        a_sq = area(3 * T, 3 * T).rearrange("p (i t) -> p i t", i=3)
        a_r = area(6 * T, 2 * T).rearrange("p (i t) -> p i t", i=2)
        o = 8 * T
        a_qtm = area(o, NT * 384).rearrange("p (t h c) -> p t h c", t=NT, h=4)
        a_ktm = area(o + NT * 384, NT * 384).rearrange("p (t h c) -> p t h c", t=NT, h=4)
        a_v = area(o + 2 * NT * 384, NT * 256).rearrange("p (t h c) -> p t h c", t=NT, h=4)
        a_kr = area(o + 2 * NT * 384 + NT * 256, NT * 32).rearrange("p (t c) -> p t c", t=NT)
        a_tmp = area(o + 2 * NT * 384 + NT * 256 + NT * 32, 4 * 16 * 16)
        a_P = area(o, 2 * T).rearrange("p (b t) -> p b t", b=2)
        a_PT = area(o + 2 * T, T)
        a_y = area(o + 3 * T, NT * 256).rearrange("p (t c) -> p t c", t=NT)
        a_sc = area(o + 3 * T + NT * 256, NT * 256)

        RAW = 4 * 772
        m_raw = area(0, RAW).rearrange("p (i t) -> p i t", i=4)
        m_W = area(0, 4 * T).rearrange("p (b d t) -> p b d t", b=2, d=2)
        m_qk = area(RAW, 4 * T).rearrange("p (i t) -> p i t", i=4)
        m_v = area(RAW + 4 * T, NT * 4 * 65).rearrange("p (t h c) -> p t h c", t=NT, h=4)
        o = RAW + 4 * T + NT * 260
        m_F = area(o, 2 * T).rearrange("p (d t) -> p d t", d=2)
        m_g = area(o + 2 * T, 2 * T).rearrange("p (d t) -> p d t", d=2)
        m_M = area(o + 4 * T, 2 * T).rearrange("p (d t) -> p d t", d=2)
        o += 6 * T
        m_tmp = area(o, T)
        m_gE = area(o + T, 192)
        m_y = area(o + T + 192, NT * 256).rearrange("p (t c) -> p t c", t=NT)
        m_sc = area(o + T + 192 + NT * 256, NT * 256)
        m_den = small[:, 640:652].rearrange("p (i t) -> p i t", i=2)
        gI, gF = YT[:, 2, 0, :], YT[:, 2, 1, :]

        g_q, g_k = area(0, T), area(T, T)
        g_lg = area(2 * T, 2 * T).rearrange("p (d t) -> p d t", d=2)
        g_t1, g_t2 = area(4 * T, T), area(5 * T, T)
        g_a = area(6 * T, 2 * T).rearrange("p (d t) -> p d t", d=2)
        g_qd = area(6 * T, T)
        g_ki = area(7 * T, T)
        g_qm = area(8 * T, 4 * T).rearrange("p (h t) -> p h t", h=4)
        g_ke = area(12 * T, T)
        g_v = area(13 * T, NT * 256).rearrange("p (t c) -> p t c", t=NT)
        g_S = area(15 * T, 12 * 256).rearrange("p (c n) -> p c n", c=12)
        g_y = area(19 * T, NT * 256).rearrange("p (t c) -> p t c", t=NT)
        g_A = area(21 * T, 512)
        g_sl = area(21 * T + 512, 256)
        g_sc = area(15 * T, NT * 256)

        d_q = area(0, 2 * T).rearrange("p (i t) -> p i t", i=2)
        d_k = area(2 * T, 2 * T).rearrange("p (i t) -> p i t", i=2)
        d_v = area(4 * T, NT * 256).rearrange("p (t h c) -> p t h c", t=NT, h=4)
        d_y = area(6 * T, NT * 256).rearrange("p (t c) -> p t c", t=NT)
        d_sc = area(8 * T, NT * 256)
        d_tm = area(8 * T, NT * 512).rearrange("p (t c) -> p t c", t=NT)
        d_tmp = area(12 * T, 4 * 256)
        d_P = area(12 * T, 4 * T).rearrange("p (b m t) -> p b m t", b=2, m=2)
        d_PT = area(16 * T, T)

        g_wbr = area(0, 8 * D).rearrange("p (i n) -> p i n", i=8)
        g_mT = area(8 * D, KD * T).rearrange("p (k t) -> p k t", k=KD)
        g_gb = area(8 * D + KD * T, 2 * 512).rearrange("p (b t) -> p b t", b=2)
        g_pb = area(8 * D + KD * T + 1024, 2 * 512).rearrange("p (b t) -> p b t", b=2)
        o_y = area(0, NT * D).rearrange("p (t d) -> p t d", t=NT)
        o_junk = area(8 * D + KD * T, 1024)
        o_row = area(8 * D + KD * T + 1024, 1024)
        o_diag = area(6 * D, 1024).rearrange("p (k c) -> p k c", k=KD)

        e_xn = area(0, NT * D).rearrange("p (t d) -> p t d", t=NT)
        o = NT * D
        e_junk = area(o, 1024)
        e_aff = area(o, 96).rearrange("p (t e) -> p t e", t=NT)
        e_pos = area(o + 96, 96).rearrange("p (t e) -> p t e", t=NT)
        o += 1024
        e_affT = area(o, T)
        e_wk = area(o + T, T)
        e_mk = area(o + 2 * T, T)
        e_cu = area(o + 3 * T, T)
        e_sel = area(o, NT * CAPS).rearrange("p (t j) -> p t j", t=NT)
        e_ta = area(o + NT * CAPS, 2 * NT).rearrange("p (t c) -> p t c", t=NT)
        o += NT * (CAPS + 2)
        e_rows = area(o, D)
        o += 4 * T - NT * (CAPS + 2)
        e_xs = area(o, KD * CAPS).rearrange("p (k j) -> p k j", k=KD)
        o += KD * CAPS
        e_hid = area(o, FF)
        o += FF
        e_hidT = area(o, NF * CAPS).rearrange("p (f j) -> p f j", f=NF)
        o += NF * CAPS
        e_sg = area(o, 2 * 512).rearrange("p (b n) -> p b n", b=2)
        e_ys = area(o + 1024, 1024)
        e_row = area(o + 2048, 1024)
        facc = YTr.rearrange("p (t d) -> p t d", t=NT)

        s_cs = small[:, 0:16].rearrange("p (k j) -> p k j", k=KD)
        s_sc = small[:, 16:32].rearrange("p (k j) -> p k j", k=KD)
        s_mod = small[:, 32:128].rearrange("p (m j) -> p m j", m=48)
        s_A = small[:, 128:160].rearrange("p (s j k) -> p s j k", s=2, j=2)
        s_G = small[:, 160:192].rearrange("p (s j k) -> p s j k", s=2, j=2)
        s_B = small[:, 192:224].rearrange("p (s j k) -> p s j k", s=2, j=2)
        s_ssq = small[:, 224:230]
        s_ms = small[:, 230:236]
        s_rt = small[:, 236:242]
        s_r = small[:, 242:248]
        s_mx = small[:, 248:256].rearrange("p (b m i) -> p b m i", b=2, m=2)
        s_nb = small[:, 256:260].rearrange("p (b m) -> p b m", b=2)
        s_sum = small[:, 260:268].rearrange("p (b m i) -> p b m i", b=2, m=2)
        s_rs = small[:, 268:272].rearrange("p (b m) -> p b m", b=2)
        s_lam = small[:, 272:280]
        s_hs = small[:, 280:376].rearrange("p (i c) -> p i c", i=4)
        s_ge = small[:, 376:400].rearrange("p (d c) -> p d c", d=2)
        s_ssq2 = small[:, 400:412].rearrange("p (i t) -> p i t", i=2)
        s_soft = small[:, 412:424].rearrange("p (i t) -> p i t", i=2)
        s_top = small[:, 424:488].rearrange("p (i c) -> p i c", i=8)
        s_cnt = small[:, 488:492]
        s_pc = small[:, 492:504].rearrange("p (i t) -> p i t", i=2)
        s_mrow = area(WORK_W - 1024, 1024).rearrange("p (b n) -> p b n", b=2)
        s_l = small[:, 512:640]
        s_sel = small[:, 504:506]

        def parts(n, cap):
            if cap != 64:
                return [(cap, 0, n)]
            return [(P, 0, n - 256)] + ([(64, n - 256, 256)] if n < 512 else [])

        block = ctx.enter_context(nc.Block())
        piece_done = {}

        PER_E = {"dve": {}, "act": {}, "pe": {}}

        @block.tensor
        def _(pe):
            c = Order(pe, sems, None)
            st = {"a": 0, "d": 0, "pv": 0}

            def job(kind):
                n = st[kind]
                start, of = rings[kind][-1]
                if n - start >= len(of):
                    pe.wait_ge(sems[kind + "_free"], n - len(of) + 1)
                st[kind] = n + 1
                return ring_bank(kind, n)

            def ring_a(of):
                pe.wait_ge(sems["a_free"], st["a"])
                rings["a"].append((st["a"], of))

            def used(n, kind="a"):
                piece_done[n] = (kind + "_done", st[kind])

            def fm(w, c0, M, off, n):
                b = job("a")
                for k in range(KD):
                    ins = pe.matmul(b[0:M, 0:n], w[:, k, c0:c0 + M], HT[:, k, off:off + n], start=(k == 0), stop=(k == KD - 1))
                ins.then_inc(sems["a_done"], 1)

            def tm(w, c0, n, t):
                b = job("a")
                for k in range(KD):
                    ins = pe.matmul(b[:, 0:n], HT[:, k, t * P:(t + 1) * P], w[:, k, c0:c0 + n], start=(k == 0), stop=(k == KD - 1))
                ins.then_inc(sems["a_done"], 1)

            def transpose_tiles(kind, src, tiles, rows=P):
                b = job(kind)
                for i, t in enumerate(tiles):
                    ins = pe.transpose(b[0:rows, i * P:(i + 1) * P], src(t), ident)
                ins.then_inc(sems[kind + "_done"], 1)

            def seg_tiles(off, n):
                return range(off // P, (off + n) // P)

            def norm_transposes(L, xn):
                pe.wait_ge(sems["xn"], c.nth("xn", 1))
                for k in range(KD):
                    for off, n in SEG:
                        transpose_tiles("a", lambda t: xn[:, t, k * P:(k + 1) * P], seg_tiles(off, n))
                pe.wait_ge(sems["a_free"], st["a"])

            def ada(L, p):
                if p < PIECES_ADA:
                    n = N_ADA[L] + p
                    pe.wait_ge(w_in[n % SLOTS], landings(n))
                    b = job("a")
                    w = slot(n)
                    for k in range(KD):
                        ins = pe.matmul(b[0:2, :], s_sc[:, k, :], w[:, k, :], start=(k == 0), stop=(k == KD - 1))
                    ins.then_inc(sems["a_done"], 1)
                    used(n)
                if p > 0:
                    pe.wait_ge(sems["mrow"], c.nth("mrow"))
                    b = job("a")
                    for m in range(4):
                        ins = pe.transpose(b[:, 2 * m:2 * m + 2], s_mrow[0:2, (p - 1) % 2, m * P:(m + 1) * P], ident[0:2, 0:2])
                    ins.then_inc(sems["a_done"], 1)

            def finish_transposes(y):
                pe.wait_ge(sems["y_ready"], c.nth("y_ready"))
                for i in range(2):
                    for off, n in QS:
                        transpose_tiles("d", lambda t: y[:, t, i * P:(i + 1) * P], seg_tiles(off, n))

            def mla(L):
                n0 = N_IN[L]
                pe.wait_ge(w_in[(n0) % SLOTS], landings(n0))
                w = slot(n0, W_IN_SPLIT[0])
                for i in range(2):
                    for off, n in QS:
                        fm(w, i * P, P, off, n)
                for off, n in SEG:
                    fm(w, 256, P, off, n)
                for t in range(NT):
                    tm(w, 384, 32, t)
                for off, n in SEG:
                    fm(w, 416, 40, off, n)
                used(n0)
                pe.wait_ge(sems["mla_sq"], c.nth("mla_sq"))
                for off, n in QS:
                    b = job("a")
                    pe.matmul(b[:, 0:n], ones, a_sq[:, 0, off:off + n], start=True, stop=False)
                    pe.matmul(b[:, 0:n], ones, a_sq[:, 1, off:off + n], start=False, stop=True).then_inc(sems["a_done"], 1)
                for off, n in SEG:
                    b = job("a")
                    pe.matmul(b[:, 0:n], ones, a_sq[:, 2, off:off + n], start=True, stop=True).then_inc(sems["a_done"], 1)
                pe.wait_ge(sems["mla_n"], c.nth("mla_n"))
                uq = pk("w_uq").rearrange("p (i n) -> p i n", i=2)
                for t in QT:
                    b = job("a")
                    for i in range(2):
                        ins = pe.matmul(b[:, 0:384], a_ql[:, i, t * P:(t + 1) * P], uq[:, i, :], start=(i == 0), stop=(i == 1))
                    ins.then_inc(sems["a_done"], 1)
                for t in range(NT):
                    b = job("a")
                    pe.matmul(b[:, :], a_kv[:, t * P:(t + 1) * P], pk("w_ukv"), start=True, stop=True).then_inc(sems["a_done"], 1)
                pe.wait_ge(sems["mla_rope"], c.nth("mla_rope"))
                for h in range(4):
                    for off, n in QS:
                        transpose_tiles("a", lambda t: a_qtm[:, t, h, :], seg_tiles(off, n), 96)
                    for off, n in SEG:
                        transpose_tiles("a", lambda t: a_ktm[:, t, h, :], seg_tiles(off, n), 96)
                ring_a((0, 1, 2, 6, 7))
                attention(L, [(h, t) for h in range(4) for t in QT], 1,
                          lambda it, m: a_qT[0:96, it[0], it[1] * P:(it[1] + 1) * P],
                          lambda it, m, off, n: a_kT[0:96, it[0], off:off + n],
                          lambda it, b: a_P[:, b, :], a_PT, a_v)
                finish_transposes(a_y)

            def attention(L, items, maps, q, k, p, PT, v):
                def scores(it):
                    for m in range(maps):
                        for off, n in key_pieces(it[1]):
                            b = job("a")
                            pe.matmul(b[:, 0:n], q(it, m), k(it, m, off, n), start=True, stop=True).then_inc(sems["a_done"], 1)
                        marks[("S", L, maps, it, m)] = st["a"]

                def turn(i, it):
                    pe.wait_ge(sems["att_p"], c.nth("att_p"))
                    if maps == 2:
                        pe.wait_ge(sems["att_a"], c.nth("att_a"))
                    keys = range(sum(n for _, n in key_pieces(it[1])) // P)
                    for first in range(0, len(keys), 4):
                        transpose_tiles("d", lambda t: p(it, i % 2)[:, t * P:(t + 1) * P], keys[first:first + 4])
                    marks[("T", L, maps, it)] = st["d"]

                def weigh(it):
                    pe.wait_ge(sems["d_free"], st["d"])
                    b = job("d")
                    keys = range(sum(n for _, n in key_pieces(it[1])) // P)
                    for t in keys:
                        ins = pe.matmul(b[:, 0:64], PT[:, t * P:(t + 1) * P], v[:, t, it[0], :],
                                        start=(t == 0), stop=(t == len(keys) - 1))
                    ins.then_inc(sems["d_done"], 1)

                scores(items[0])
                scores(items[1])
                for i, it in enumerate(items):
                    turn(i, it)
                    if i + 2 < len(items):
                        scores(items[i + 2])
                    weigh(it)
                    if maps == 2 and L + 1 < DEPTH and i % 2 == 1:
                        ada(L + 1, i // 2)
                if maps == 2 and L + 1 < DEPTH:
                    ada(L + 1, PIECES_ADA)
                ring_a((0, 1, 2))

            def mlstm(L):
                n0 = N_IN[L] + 1
                pe.wait_ge(w_in[(n0) % SLOTS], landings(n0))
                w = slot(n0)
                for i in range(4):
                    for off, n in (QS if i < 2 else SEG):
                        fm(w, i * P, P, off, n)
                used(n0)
                pe.wait_ge(w_in[(n0 + 1) % SLOTS], landings(n0 + 1))
                w = slot(n0 + 1)
                for t in range(NT):
                    tm(w, 0, 512 if t in QT else 256, t)
                used(n0 + 1)
                pe.wait_ge(sems["ml_rows"], c.nth("ml_rows"))
                b = job("d")
                for part, src in enumerate((m_g, m_F)):
                    for d in range(2):
                        for t in range(NT):
                            at = part * 96 + (d * NT + t) * 8
                            ins = pe.transpose(b[:, at:at + 8], src[0:8, d, t * P:(t + 1) * P], ident[0:8, 0:8])
                ins.then_inc(sems["d_done"], 1)
                pe.wait_ge(sems["ml_qk"], c.nth("ml_qk"))
                rows = cc("rows")

                def products(h, j):
                    hp = (h % 2) * 64
                    for off, n in (QS if j < CT else QS[:1]):
                        b = job("d")
                        pe.matmul(b[:, 0:n], m_qk[hp:hp + 64, 2 + h // 2, j * P:(j + 1) * P],
                                       m_qk[hp:hp + 64, h // 2, off:off + n], start=True, stop=True).then_inc(sems["d_done"], 1)

                for h in range(4):
                    for d in range(2):
                        b = job("a")
                        pe.matmul(b[:, :], rows[0:8, (4 * d + h) * P:(4 * d + h + 1) * P], m_M[0:8, d, CTX:T],
                                       start=True, stop=True).then_inc(sems["a_done"], 1)
                    if len(QS) == 2:
                        b = job("a")
                        for d in range(2):
                            ins = pe.matmul(b[:, d * CTX:(d + 1) * CTX], rows[0:8, (4 * d + h) * P:(4 * d + h + 1) * P],
                                            m_M[0:8, d, 0:CTX], start=True, stop=True)
                        ins.then_inc(sems["a_done"], 1)
                    products(h, 0)
                    for j in range(NT):
                        if j + 1 < NT:
                            products(h, j + 1)
                        pe.wait_ge(sems["ml_s"], c.nth("ml_s"))
                        if j == 0 and h >= 1:
                            pe.wait_ge(sems["x_free"], c.nth("x_free"))
                        for d in range(2):
                            ts = ml_tiles(L, d, j)
                            for t in ts:
                                ins = pe.matmul(banks[6 + d][:, t * 65:t * 65 + 65], m_W[:, j % 2, d, t * P:(t + 1) * P],
                                                m_v[:, j, h, :], start=(j == 0 and t == ts[0]),
                                                stop=(j == ml_last(d, t)), skip_group_check=True)
                        ins.then_inc(sems["pv_done"], 1)
                pe.wait_ge(sems["x_free"], c.nth("x_free"))
                finish_transposes(m_y)

            def gla(L):
                n0 = N_IN[L] + 3
                pe.wait_ge(w_in[(n0) % SLOTS], landings(n0))
                w = slot(n0, W_IN_SPLIT[3])
                for off, n in SEG:
                    fm(w, 0, 48, off, n)
                for off, n in QS:
                    fm(w, 48, P, off, n)
                for off, n in SEG:
                    fm(w, 48 + P, P, off, n)
                used(n0)
                pe.wait_ge(w_in[(n0 + 1) % SLOTS], landings(n0 + 1))
                w = slot(n0 + 1)
                for t in range(NT):
                    tm(w, 0, 512 if t in QT else 256, t)
                used(n0 + 1)
                pe.wait_ge(sems["a_free"], st["a"])
                wa = pk("w_alpha").rearrange("p (d n) -> p d n", d=2)
                for d in range(2):
                    for off, n in SEG:
                        b = job("a")
                        pe.matmul(b[:, 0:n], wa[0:16, d, :], g_a[0:16, d, off:off + n], start=True, stop=True).then_inc(sems["a_done"], 1)
                for d in range(2):
                    pe.wait_ge(sems["gl_ops"], c.nth("gl_ops"))
                    for off, n in SEG:
                        transpose_tiles("d", lambda t: g_t1[:, t * P:(t + 1) * P], seg_tiles(off, n))
                    pe.wait_ge(sems["d_free"], st["d"])
                    for i in range(11):
                        ch = gla_chunk(d, i)
                        t, r = ch // 2, (ch % 2) * 64
                        b = job("d")
                        pe.matmul(b[:, 0:256], g_ke[r:r + 64, t * P:(t + 1) * P], g_v[r:r + 64, t, :],
                                       start=True, stop=True).then_inc(sems["d_done"], 1)
                    pe.wait_ge(sems["gl_state"], c.nth("gl_state"))

                    def scores(t):
                        b = job("d")
                        pe.matmul(b[:, :].rearrange("p (h c) -> p h c", h=4), g_ki[:, t * P:(t + 1) * P],
                                       g_qm[:, :, t * P:(t + 1) * P], start=True, stop=True).then_inc(sems["d_done"], 1)

                    for t in QT:
                        scores(t)
                        pe.wait_ge(sems["gl_att"], c.nth("gl_att"))
                        b = job("d")
                        for r in range(2):
                            pe.matmul(b[r * 64:r * 64 + 64, 0:256], g_qd[:, t * P + r * 64:t * P + r * 64 + 64],
                                      g_S[:, 2 * t + r, :], start=True, stop=False, skip_group_check=True)
                        for h in range(4):
                            ins = pe.matmul(b[:, h * 64:h * 64 + 64], g_A[:, h * P:(h + 1) * P],
                                            g_v[:, t, h * 64:h * 64 + 64], start=False, stop=True, skip_group_check=True)
                        ins.then_inc(sems["d_done"], 1)
                finish_transposes(g_y)

            def diff(L):
                n0 = N_IN[L] + 5
                pe.wait_ge(w_in[(n0) % SLOTS], landings(n0))
                w = slot(n0)
                for t in range(NT):
                    tm(w, 0, 512, t)
                used(n0)
                pe.wait_ge(w_in[(n0 + 1) % SLOTS], landings(n0 + 1))
                w = slot(n0 + 1, 256)
                for t in range(NT):
                    tm(w, 0, 256, t)
                used(n0 + 1)
                pe.wait_ge(sems["mla_rope"], c.nth("mla_rope"))
                for i in range(2):
                    for off, n in QS:
                        transpose_tiles("a", lambda t: d_tm[:, t, i * P:(i + 1) * P], seg_tiles(off, n))
                    for off, n in SEG:
                        transpose_tiles("a", lambda t: d_tm[:, t, 256 + i * P:256 + (i + 1) * P], seg_tiles(off, n))
                ring_a((0, 1, 2, 6, 7))

                def q(it, m):
                    g = it[0] * 2 + m
                    return d_q[(g % 4) * 32:(g % 4) * 32 + 32, g // 4, it[1] * P:(it[1] + 1) * P]

                def k(it, m, off, n):
                    g = it[0] * 2 + m
                    return d_k[(g % 4) * 32:(g % 4) * 32 + 32, g // 4, off:off + n]

                attention(L, [(h, t) for h in range(4) for t in QT], 2, q, k, lambda it, b: d_P[:, b, 0, :], d_PT, d_v)
                finish_transposes(d_y)

            def merge(L):
                pe.wait_ge(sems["d_free"], st["d"])
                n0 = N_MERGE[L]
                pe.wait_ge(sems["pack_in"], 16 * (2 * L + 2))
                for half in range(2):
                    for n_ in range(4):
                        n = n0 + half * 4 + n_
                        pe.wait_ge(w_in[(n) % SLOTS], landings(n))
                        w = slot(n)
                        for d4 in range(4):
                            dt = half * 4 + d4
                            for off, ln in QS:
                                fm(w, d4 * P, P, off, ln)
                                b = job("d")
                                for i in range(2):
                                    ins = pe.matmul(b[:, 0:ln], g_wbr[:, 2 * n_ + i, dt * P:(dt + 1) * P],
                                                    YT[:, n_, i, off:off + ln], start=(i == 0), stop=(i == 1))
                                ins.then_inc(sems["d_done"], 1)
                        used(n)
                pe.wait_ge(sems["mg_sum"], c.nth("mg_sum"))
                for half in range(2):
                    n = n0 + 8 + half
                    pe.wait_ge(w_in[(n) % SLOTS], landings(n))
                    w = slot(n)
                    for t in QT:
                        b = job("a")
                        for k in range(KD):
                            ins = pe.matmul(b[:, :], g_mT[:, k, t * P:(t + 1) * P], w[:, k, :], start=(k == 0), stop=(k == KD - 1))
                        ins.then_inc(sems["a_done"], 1)
                    used(n)

            def gate_rows(diag):
                for _ in QS:
                    pe.wait_ge(sems["diag"], c.nth("diag"))
                    for half in range(2):
                        b = job("a")
                        for k in range(4):
                            ins = pe.matmul(b[:, k * P:(k + 1) * P], ones, diag[:, half * 4 + k, :], start=True, stop=True)
                        ins.then_inc(sems["a_done"], 1)

            def moe(L):
                router = pk("w_router").rearrange("p (k e) -> p k e", k=KD)
                b = job("d")
                for t in QT:
                    for k in range(KD):
                        ins = pe.matmul(b[:, t * NE:(t + 1) * NE], HT[:, k, t * P:(t + 1) * P], router[:, k, :],
                                        start=(k == 0), stop=(k == KD - 1))
                ins.then_inc(sems["d_done"], 1)
                pe.wait_ge(sems["aff"], c.nth("aff"))
                for off, n in QS:
                    b = job("d")
                    for i, t in enumerate(seg_tiles(off, n)):
                        ins = pe.transpose(b[0:NE, i * P:(i + 1) * P], e_aff[:, t, :], ident)
                    ins.then_inc(sems["d_done"], 1)
                pe.wait_ge(sems["pos"], c.nth("pos"))
                b = job("d")
                for t in QT:
                    ins = pe.transpose(b[:, t * NE:(t + 1) * NE], e_mk[0:NE, t * P:(t + 1) * P], ident[0:NE, 0:NE])
                ins.then_inc(sems["d_done"], 1)
                pe.wait_ge(sems["a_free"], st["a"])
                pe.wait_ge(sems["d_free"], st["d"])
                cap = CAPS if len(QS) == 2 else CAP_L
                two = cap == 64
                n0 = N_EXP[L]

                def choose():
                    pe.wait_ge(sems["sel"], c.nth("sel"))
                    for t in QT:
                        ins = pe.matmul(banks[5][0:cap, 0:2], e_sel[:, t, 0:cap], e_ta[:, t, :], start=(t == QT[0]), stop=(t == QT[-1]))
                    if two:
                        for t in QT:
                            ins = pe.matmul(banks[5][64:64 + cap, 0:2], e_sel[:, t, 0:cap], e_ta[:, t, :],
                                            start=(t == QT[0]), stop=(t == QT[-1]))
                    ins.then_inc(sems["chosen"], 1)

                def turn_rows():
                    pe.wait_ge(sems["rows_in"], c.nth("rows_in", 16))
                    pe.nop(nofuse=True)
                    for k in range(KD):
                        ins = pe.transpose(banks[2 + k // 4][:, (k % 4) * cap:(k % 4 + 1) * cap], e_rows[0:cap, k * P:(k + 1) * P],
                                           ident[0:cap, 0:cap])
                    ins.then_inc(sems["rows_t"], 1)

                def expert(e, last):
                    def wpiece(i):
                        n = n0 + i
                        pe.wait_ge(sems[f"w_in{n % SLOTS}"], (e * 3 + (n // SLOTS + 1)) * 16)

                    def gate_up(g):
                        for u in range(2):
                            wpiece(2 * g + u)
                            n = EXP_W[2 * g + u]
                            w = slot(n0 + 2 * g + u, n)
                            for k in range(KD if two else 0):
                                b = banks[(0, 2, 0)[g] + u]
                                pe.matmul(b[0:64, 0:256], e_xs[:, k, 0:64], w[:, k, 0:256], start=(k == 0), stop=(k == KD - 1))
                                ins = pe.matmul(b[64:128, 0:n - 256], e_xs[:, k, 0:64], w[:, k, 256:n],
                                                start=(k == 0), stop=(k == KD - 1))
                            for k in range(0 if two else KD):
                                ins = pe.matmul(banks[(0, 2, 0)[g] + u][0:cap, 0:n], e_xs[:, k, 0:cap], w[:, k, :],
                                                start=(k == 0), stop=(k == KD - 1))
                            ins.then_inc(sems["gu"], 1)

                    def turn_hidden(g):
                        pe.wait_ge(sems["hid"], c.nth("hid"))
                        pe.nop(nofuse=True)
                        b = banks[(4, 5, 4)[g]]
                        for j in range(2 if two else 0):
                            rows = P if 4 * g + 2 + j < NF else 64
                            ins = pe.transpose(b[:, j * P:j * P + rows], e_hid[0:rows, 512 * g + j * P:512 * g + (j + 1) * P],
                                               ident[0:rows, 0:rows])
                        for i, f in enumerate(range(4 * g, min(4 * g + 4, NF)) if not two else ()):
                            ins = pe.transpose(banks[(4, 5, 4)[g]][:, i * cap:(i + 1) * cap], e_hid[0:cap, f * P:(f + 1) * P],
                                               ident[0:cap, 0:cap])
                        ins.then_inc(sems["hid_t"], 1)

                    def down(i):
                        pe.wait_ge(sems["hid_f"], c.nth("hid_f"))
                        wpiece(6 + i)
                        kk = EXP_DOWN[i]
                        w = slot(n0 + 6 + i, 1024, kk)
                        for k in range(kk):
                            f = 4 * i + k
                            at = 4 * i + ((0, 2, 1, 3)[k] if two else k)
                            for half in range(2):
                                lo = 64 * half if two else 0
                                ins = pe.matmul(banks[6 + half][lo:lo + cap, :], e_hidT[:, at, 0:cap], w[:, k, half * 512:half * 512 + 512],
                                                start=(f == 0), stop=(f == NF - 1))
                        ins.then_inc(sems["ys"], 1)

                    pe.wait_ge(sems["xs"], c.nth("xs"))
                    gate_up(0)
                    if not last:
                        choose()
                    gate_up(1)
                    turn_hidden(0)
                    gate_up(2)
                    if not last:
                        pe.wait_ge(sems["idx_next"], c.nth("idx_next"))
                    turn_hidden(1)
                    if not last:
                        turn_rows()
                    pe.wait_ge(sems["ys_a"], c.nth("ys_a"))
                    pe.wait_ge(sems["ys_d"], c.nth("ys_d"))
                    down(0)
                    turn_hidden(2)
                    down(1)
                    down(2)

                choose()
                turn_rows()
                pe.wait_ge(sems["idx_next"], c.nth("idx_next"))
                per = {"xs": 1, "sel": 1, "idx_next": 1, "rows_in": 16, "ys_a": 1, "ys_d": 1, "hid": 3, "hid_f": 3}
                with pe.Fori(0, NE - 1) as e:
                    c.begin(e, per)
                    expert(e, False)
                    c.e = None
                c.finish_loop(NE - 1)
                expert(NE - 1, True)
                pe.wait_ge(sems["ys_a"], c.nth("ys_a"))
                pe.wait_ge(sems["ys_d"], c.nth("ys_d"))

            pe.wait_ge(sems["const_in"], 16)
            for L in range(DEPTH):
                SEG, QS, QT = segs(L), segs(L, True), qtiles(L)
                pe.wait_ge(sems["pack_in"], 16 * (2 * L + 1))
                if L == 0:
                    pe.wait_ge(sems["silc"], c.nth("silc"))
                    for p in range(PIECES_ADA + 1):
                        ada(L, p)
                norm_transposes(L, V_N["xn"].rearrange("p (t d) -> p t d", t=NT))
                mla(L)
                mlstm(L)
                gla(L)
                diff(L)
                merge(L)
                gate_rows(o_diag)
                QALL, SEG = SEG, QS
                norm_transposes(L, e_xn)
                moe(L)
                gate_rows(o_diag)
            marks["a_total"] = st["a"]

        @block.scalar
        def _(act):
            c = Order(act, sems, "act_order")
            st = {"a": 0}

            def do(*a, **kw):
                c.seq(act.activation(*a, **kw))

            def copy(dst, src):
                c.seq(act.activation(dst, src, AF.Copy))

            def bank():
                return ring_bank("a", c.n["a_done"] - 1)

            def ada(p):
                if p < PIECES_ADA:
                    act.wait_ge(sems["a_done"], c.nth("a_done"))
                    b = bank()
                    copy(s_mrow[0:2, p % 2, :], b[0:2, :])
                    act.sem_inc(sems["a_free"], 1)
                    act.sem_inc(sems["mrow"], 1)
                if p > 0:
                    act.wait_ge(sems["a_done"], c.nth("a_done"))
                    b = bank()
                    copy(s_mod[:, 4 * p - 4:4 * p, :], b[:, 0:8].rearrange("p (m j) -> p m j", m=4))
                    act.sem_inc(sems["a_free"], 1)
                if p == PIECES_ADA:
                    act.sem_inc(sems["mod"], 1)

            def norm_stats(L, junk, tiles, first):
                if not first:
                    act.wait_ge(sems["layer_done"], c.nth("layer_done"))
                for t in tiles:
                    do(junk, X[:, t, :], AF.Square, accum_out=s_ssq[:, t:t + 1])
                act.sem_inc(sems["ssq"], 1)
                root("ms", s_rt, s_ms, "rt")

            def root(need, dst, src, ready):
                act.wait_ge(sems[need], c.nth(need))
                do(dst, src, AF.Sqrt)
                act.sem_inc(sems[ready], 1)

            def norm_mod(L, s):
                for k in range(KD):
                    for off, n in SEG:
                        act.wait_ge(sems["a_done"], c.nth("a_done"))
                        b = bank()
                        j = 0 if off else 1
                        do(HT[:, k, off:off + n], b[:, 0:n], AF.Identity, scale=s_A[:, s, j, k:k + 1], bias=s_B[:, s, j, k:k + 1])
                        act.sem_inc(sems["a_free"], 1)

            def softplus_parts(dst, src, need, ready):
                act.wait_ge(sems[need], c.nth(need))
                do(dst, src, AF.Abs)
                do(dst, dst, AF.Exp, scale=-1.0)
                do(dst, dst, AF.Ln, bias=ones[0:dst.shape[0], 0:1])
                act.sem_inc(sems[ready], 1)

            def mla(L):
                for i in range(2):
                    for off, n in QS:
                        act.wait_ge(sems["a_done"], c.nth("a_done"))
                        b = bank()
                        copy(a_ql[:, i, off:off + n], b[:, 0:n])
                        act.sem_inc(sems["a_free"], 1)
                for off, n in SEG:
                    act.wait_ge(sems["a_done"], c.nth("a_done"))
                    b = bank()
                    copy(a_kv[:, off:off + n], b[:, 0:n])
                    act.sem_inc(sems["a_free"], 1)
                for t in range(NT):
                    act.wait_ge(sems["a_done"], c.nth("a_done"))
                    b = bank()
                    copy(a_kr[:, t, :], b[:, 0:32])
                    act.sem_inc(sems["a_free"], 1)
                for off, n in SEG:
                    act.wait_ge(sems["a_done"], c.nth("a_done"))
                    b = bank()
                    copy(gI[0:8, off:off + n], b[0:8, 0:n])
                    copy(gF[0:8, off:off + n], b[32:40, 0:n])
                    act.sem_inc(sems["a_free"], 1)
                act.sem_inc(sems["mla_lat"], 1)
                for off, n in QS:
                    act.wait_ge(sems["a_done"], c.nth("a_done"))
                    b = bank()
                    do(a_r[:, 0, off:off + n], b[:, 0:n], AF.Sqrt, scale=1.0 / 256, bias=cc("eps"))
                    act.sem_inc(sems["a_free"], 1)
                for off, n in SEG:
                    act.wait_ge(sems["a_done"], c.nth("a_done"))
                    b = bank()
                    do(a_r[:, 1, off:off + n], b[:, 0:n], AF.Sqrt, scale=1.0 / 128, bias=cc("eps"))
                    act.sem_inc(sems["a_free"], 1)
                act.sem_inc(sems["mla_r"], 1)
                for t in QT:
                    act.wait_ge(sems["a_done"], c.nth("a_done"))
                    b = bank()
                    copy(a_qtm[:, t, :, :], b[:, 0:384].rearrange("p (h c) -> p h c", h=4))
                    act.sem_inc(sems["a_free"], 1)
                for t in range(NT):
                    act.wait_ge(sems["a_done"], c.nth("a_done"))
                    b = bank()[:, :].rearrange("p (h c) -> p h c", h=4)
                    copy(a_ktm[:, t, :, 0:64], b[:, :, 0:64])
                    copy(a_v[:, t, :, :], b[:, :, 64:128])
                    act.sem_inc(sems["a_free"], 1)
                act.sem_inc(sems["mla_tm"], 1)
                for h in range(4):
                    for off, n in QS:
                        act.wait_ge(sems["a_done"], c.nth("a_done"))
                        b = bank()
                        copy(a_qT[0:96, h, off:off + n], b[0:96, 0:n])
                        act.sem_inc(sems["a_free"], 1)
                    for off, n in SEG:
                        act.wait_ge(sems["a_done"], c.nth("a_done"))
                        b = bank()
                        copy(a_kT[0:96, h, off:off + n], b[0:96, 0:n])
                        act.sem_inc(sems["a_free"], 1)
                softmax(L, [(h, t) for h in range(4) for t in QT], 1, lambda b, m: a_P[:, b, :], 96 ** -0.5)
                finish()

            def softmax(L, items, maps, p, scale):
                with_ada = maps == 2 and L + 1 < DEPTH
                for i, it in enumerate(items):
                    if with_ada and i >= 4 and i % 2 == 0:
                        ada((i - 4) // 2)
                    if i >= 2 and maps == 1:
                        act.wait_ge(sems["d_done"], marks[("T", L, maps, items[i - 2])])
                    if i >= 2 and maps == 2:
                        act.wait_ge(sems["d_done"], marks[("T", L, maps, items[i - 2])])
                    for m in range(maps):
                        act.wait_ge(sems["att_max"], c.nth("att_max"))
                        for x, (off, n) in enumerate(key_pieces(it[1])):
                            act.wait_ge(sems["a_done"], c.nth("a_done"))
                            b = bank()
                            do(p(i % 2, m)[:, x * 512:x * 512 + n], b[:, 0:n], AF.Exp, scale=scale,
                               bias=s_nb[:, i % 2, m:m + 1], accum_out=s_sum[:, i % 2, m, x:x + 1])
                            act.sem_inc(sems["a_free"], 1)
                    act.sem_inc(sems["att_p"], 1)
                if with_ada:
                    for p in range(PIECES_ADA - 2, PIECES_ADA + 1):
                        ada(p)

            def finish():
                root("hs_ms", s_hs[:, 2, :], s_hs[:, 1, :], "hs_rt")
                act.wait_ge(sems["branch_done"], c.nth("branch_done"))

            def mlstm(L):
                for i in range(4):
                    for off, n in (QS if i < 2 else SEG):
                        act.wait_ge(sems["a_done"], c.nth("a_done"))
                        b = bank()
                        at = 1 if off == 0 else 259
                        copy(m_raw[:, i, at:at + n], b[:, 0:n])
                        act.sem_inc(sems["a_free"], 1)
                act.sem_inc(sems["ml_raw"], 1)
                for t in range(NT):
                    act.wait_ge(sems["a_done"], c.nth("a_done"))
                    b = bank()
                    copy(m_v[:, t, :, 0:64], b[:, 0:256].rearrange("p (h c) -> p h c", h=4))
                    if t in QT:
                        do(YT[:, 1, t // 3, (t % 3) * 256:(t % 3) * 256 + 256], b[:, 256:512], AF.Sigmoid)
                    act.sem_inc(sems["a_free"], 1)
                act.wait_ge(sems["ml_conv"], c.nth("ml_conv"))
                do(m_qk[:, :, CTX:T], m_qk[:, :, CTX:T], AF.Silu)
                k0 = 0 if len(QS) == 2 else 2
                do(m_qk[:, k0:4, 0:CTX], m_qk[:, k0:4, 0:CTX], AF.Silu)
                act.sem_inc(sems["ml_qk"], 1)
                softplus_parts(m_F[0:8, 0, :], gF[0:8, :], "ml_x", "ml_l")
                act.wait_ge(sems["ml_m"], c.nth("ml_m"))
                do(m_F[0:8, :, :], m_F[0:8, :, :], AF.Exp, scale=-1.0)
                act.sem_inc(sems["ml_rows"], 1)
                act.wait_ge(sems["ml_e"], c.nth("ml_e"))
                for h in range(4):
                    mb = {}
                    for d in range(2):
                        act.wait_ge(sems["a_done"], c.nth("a_done"))
                        mb[(d, 1)] = bank()[:, :]
                    if len(QS) == 2:
                        act.wait_ge(sems["a_done"], c.nth("a_done"))
                        b = bank()
                        for d in range(2):
                            mb[(d, 0)] = b[:, d * CTX:(d + 1) * CTX]
                    for j in range(NT):
                        i = (L * 4 + h) * NT + j
                        if i >= 2:
                            act.wait_ge(sems["pv_done"], i - 1)
                        for d in range(2):
                            ts = ml_tiles(L, d, j)
                            for lat, (lo, hi) in enumerate(((0, CT), (CT, NT))):
                                r = [t for t in ts if lo <= t < hi]
                                if r:
                                    a, z = r[0] * P, (r[-1] + 1) * P
                                    do(m_W[:, j % 2, d, a:z], mb[(d, lat)][:, a - lo * P:z - lo * P], AF.Exp, scale=-1.0,
                                       bias=m_gE[:, (d * NT + j) * 8 + 4 * d + h:(d * NT + j) * 8 + 4 * d + h + 1])
                        act.sem_inc(sems["ml_w"], 1)
                    for _ in range(3 if len(QS) == 2 else 2):
                        act.sem_inc(sems["a_free"], 1)
                finish()

            def gla(L):
                for off, n in SEG:
                    act.wait_ge(sems["a_done"], c.nth("a_done"))
                    b = bank()
                    copy(g_a[0:16, 0, off:off + n], b[0:16, 0:n])
                    copy(g_a[0:16, 1, off:off + n], b[32:48, 0:n])
                    act.sem_inc(sems["a_free"], 1)
                for off, n in QS:
                    act.wait_ge(sems["a_done"], c.nth("a_done"))
                    b = bank()
                    copy(g_q[:, off:off + n], b[:, 0:n])
                    act.sem_inc(sems["a_free"], 1)
                for off, n in SEG:
                    act.wait_ge(sems["a_done"], c.nth("a_done"))
                    b = bank()
                    copy(g_k[:, off:off + n], b[:, 0:n])
                    act.sem_inc(sems["a_free"], 1)
                for t in range(NT):
                    act.wait_ge(sems["a_done"], c.nth("a_done"))
                    b = bank()
                    copy(g_v[:, t, :], b[:, 0:256])
                    if t in QT:
                        do(YT[:, 2, t // 3, (t % 3) * 256:(t % 3) * 256 + 256], b[:, 256:512], AF.Silu)
                    act.sem_inc(sems["a_free"], 1)
                for d in range(2):
                    for off, n in SEG:
                        act.wait_ge(sems["a_done"], c.nth("a_done"))
                        b = bank()
                        do(g_lg[:, d, off:off + n], b[:, 0:n], AF.Identity, bias=pk("b_alpha")[:, d:d + 1])
                        act.sem_inc(sems["a_free"], 1)
                act.sem_inc(sems["gl_in"], 1)
                for d in range(2):
                    do((g_t1, g_t2)[d], g_lg[:, d, :], AF.Abs)
                    do((g_t1, g_t2)[d], (g_t1, g_t2)[d], AF.Exp, scale=-1.0)
                    do((g_t1, g_t2)[d], (g_t1, g_t2)[d], AF.Ln, bias=ones[:, 0:1])
                act.sem_inc(sems["gl_l"], 1)
                for d in range(2):
                    act.wait_ge(sems["gl_g"], c.nth("gl_g"))
                    do(g_t1, g_t1, AF.Exp)
                    do(g_t2, g_lg[:, d, :], AF.Exp, scale=-1.0)
                    do(g_lg[:, d, :], g_lg[:, d, :], AF.Exp)
                    do(s_ge[:, d, :], s_ge[:, d, :], AF.Exp)
                    act.sem_inc(sems["gl_e"], 1)
                finish()

            def diff(L):
                act.wait_ge(sems["lam_p"], c.nth("lam_p"))
                do(s_lam[:, 2:4], s_lam[:, 0:2], AF.Exp)
                act.sem_inc(sems["lam_e"], 1)
                for t in range(NT):
                    act.wait_ge(sems["a_done"], c.nth("a_done"))
                    b = bank()
                    copy(d_tm[:, t, :], b[:, :])
                    act.sem_inc(sems["a_free"], 1)
                for t in range(NT):
                    act.wait_ge(sems["a_done"], c.nth("a_done"))
                    b = bank()
                    copy(d_v[:, t, :, :], b[:, 0:256].rearrange("p (h c) -> p h c", h=4))
                    act.sem_inc(sems["a_free"], 1)
                act.sem_inc(sems["mla_tm"], 1)
                for i in range(2):
                    for off, n in QS:
                        act.wait_ge(sems["a_done"], c.nth("a_done"))
                        b = bank()
                        copy(d_q[:, i, off:off + n], b[:, 0:n])
                        act.sem_inc(sems["a_free"], 1)
                    for off, n in SEG:
                        act.wait_ge(sems["a_done"], c.nth("a_done"))
                        b = bank()
                        copy(d_k[:, i, off:off + n], b[:, 0:n])
                        act.sem_inc(sems["a_free"], 1)
                softmax(L, [(h, t) for h in range(4) for t in QT], 2, lambda b, m: d_P[:, b, m, :], 32 ** -0.5)
                finish()

            def merge(L):
                i = 0
                for half in range(2):
                    for n_ in range(4):
                        for d4 in range(4):
                            for off, ln in QS:
                                act.wait_ge(sems["a_done"], c.nth("a_done"))
                                b = bank()
                                if i >= 2:
                                    act.wait_ge(sems["mg_prod"], c.nth("mg_prod"))
                                do(g_gb[:, i % 2, 0:ln], b[:, 0:ln], AF.Sigmoid,
                                   bias=pk("b_gate")[:, n_ * 8 + half * 4 + d4:n_ * 8 + half * 4 + d4 + 1])
                                act.sem_inc(sems["a_free"], 1)
                                act.sem_inc(sems["gate"], 1)
                                i += 1
                act.wait_ge(sems["mg_prod"], c.nth("mg_prod", 2))
                for half in range(2):
                    for t in QT:
                        act.wait_ge(sems["a_done"], c.nth("a_done"))
                        b = bank()
                        do(o_junk[:, 0:512], b[:, :], AF.Square, accum_out=s_ssq2[:, half, t:t + 1])
                        copy(o_y[:, t, half * 512:half * 512 + 512], b[:, :])
                        act.sem_inc(sems["a_free"], 1)
                act.sem_inc(sems["yo"], 1)
                root("ms", s_rt, s_ms, "rt")
                rows(o_row)

            def rows(row):
                for i in range(len(QS)):
                    if i:
                        act.wait_ge(sems["row_free"], c.nth("row_free"))
                    for half in range(2):
                        act.wait_ge(sems["a_done"], c.nth("a_done"))
                        b = bank()
                        copy(row[:, half * 512:half * 512 + 512], b[:, :])
                        act.sem_inc(sems["a_free"], 1)
                    act.sem_inc(sems["grow"], 1)

            def moe(L):
                act.wait_ge(sems["rt_max"], c.nth("rt_max"))
                do(e_aff[:, QT[0]:NT, :], e_aff[:, QT[0]:NT, :], AF.Exp)
                act.sem_inc(sems["rt_exp"], 1)
                cap = CAPS if len(QS) == 2 else CAP_L

                def hidden(g):
                    act.wait_ge(sems["gu"], c.nth("gu"))
                    n = EXP_W[2 * g]
                    for rows, c0, c1 in parts(n, cap):
                        do(e_sg[0:rows, g % 2, c0:c1], banks[(0, 2, 0)[g]][0:rows, c0:c1], AF.Silu)
                    act.sem_inc(sems["silu"], 1)
                    c.nth("gu")

                def turned(g):
                    act.wait_ge(sems["hid_t"], c.nth("hid_t"))
                    n = min(4, NF - 4 * g)
                    copy(e_hidT[:, 4 * g:4 * g + n, 0:cap], banks[(4, 5, 4)[g]][:, 0:n * cap].rearrange("p (f j) -> p f j", f=n))
                    act.sem_inc(sems["hid_f"], 1)

                def expert():
                    hidden(0)
                    hidden(1)
                    turned(0)
                    hidden(2)
                    turned(1)
                    turned(2)
                    act.wait_ge(sems["idx_now"], c.nth("idx_now"))
                    act.wait_ge(sems["ys"], c.nth("ys", 3))
                    do(e_ys[0:cap, 0:512], banks[6][0:cap, :], AF.Copy, scale=s_sel[0:cap, 1:2])
                    act.sem_inc(sems["ys_a"], 1)

                act.sem_inc(sems["ys_a"], 1)
                per = {"gu": 6, "hid_t": 3, "idx_now": 1, "ys": 3, "act_order": 7 + (cap == 64)}
                with act.Fori(0, NE) as e:
                    c.begin(e, per)
                    expert()
                    c.e = None
                c.finish_loop(NE)
                for t in QT:
                    if t == QT[0]:
                        act.wait_ge(sems["f_back"], c.nth("f_back", 16))
                    do(e_junk, facc[:, t, :], AF.Square, accum_out=s_ssq[:, t:t + 1])
                act.sem_inc(sems["ssq"], 1)
                root("ms", s_rt, s_ms, "rt")
                rows(e_row)

            act.wait_ge(sems["const_in"], 16)
            act.wait_ge(sems["x_in"], 48)
            for L in range(DEPTH):
                SEG, QS, QT = segs(L), segs(L, True), qtiles(L)
                act.wait_ge(sems["pack_in"], 16 * (2 * L + 1))
                if L == 0:
                    do(s_sc, s_cs, AF.Silu)
                    act.sem_inc(sems["silc"], 1)
                    for p in range(PIECES_ADA + 1):
                        ada(p)
                norm_stats(L, V_N["junk"], range(NT), L == 0)
                norm_mod(L, 0)
                mla(L)
                mlstm(L)
                gla(L)
                diff(L)
                merge(L)
                SEG = QS
                norm_stats(L, e_junk, QT, False)
                norm_mod(L, 1)
                moe(L)

        @block.vector
        def _(dve):
            c = Order(dve, sems, "dve_order")
            st = {"d": 0}
            S = c.seq

            def bank():
                return ring_bank("d", c.n["d_done"] - 1)

            def tt(o_, a, b, op):
                S(dve.tensor_tensor(o_, a, b, op))

            def ts(o_, a, s1, op0, s2=None, op1=None):
                if op1 is None:
                    S(dve.tensor_scalar(o_, a, s1, None, op0))
                else:
                    S(dve.tensor_scalar(o_, a, s1, s2, op0, op1))

            def copy(o_, a):
                S(dve.tensor_copy(o_, a))

            def stt(o_, a, s, b, op0, op1):
                S(dve.scalar_tensor_tensor(out=o_, in0=a, scalar=s, in1=b, op0=op0, op1=op1))

            def scan(o_, a, b, init, op0, op1):
                S(dve.tensor_tensor_scan(o_, a, b, init, op0, op1))

            def norm_apply(xn, tiles, src):
                dve.wait_ge(sems["ssq"], c.nth("ssq"))
                t0 = tiles[0]
                ts(s_ms[:, t0:NT], s_ssq[:, t0:NT], 1.0 / D, ALU.mult, EPS, ALU.add)
                dve.sem_inc(sems["ms"], 1)
                dve.wait_ge(sems["rt"], c.nth("rt"))
                S(dve.reciprocal(s_r[:, t0:NT], s_rt[:, t0:NT]))
                if xn is not None:
                    for t in tiles:
                        ts(xn[:, t, :], src[:, t, :], s_r[:, t:t + 1], ALU.mult)
                    dve.sem_inc(sems["xn"], 1)

            def modulation(L):
                dve.wait_ge(sems["mod"], c.nth("mod"))
                b_ada = pk("b_ada").unsqueeze(2).to_broadcast([P, 48, 2])
                tt(s_mod, s_mod, b_ada, ALU.add)
                for s in range(2):
                    pre = pk(("g_mix_pre", "g_ffn_pre")[s])
                    post = pk(("g_mix_post", "g_ffn_post")[s])
                    for j in range(2):
                        stt(s_A[:, s, j, :], s_mod[:, 24 * s + 8:24 * s + 16, j], 1.0, pre, ALU.add, ALU.mult)
                        tt(s_G[:, s, j, :], s_mod[:, 24 * s + 16:24 * s + 24, j], post, ALU.mult)
                        copy(s_B[:, s, j, :], s_mod[:, 24 * s:24 * s + 8, j])

            def rope(x, t, groups, tmp):
                def tab(name):
                    v = cc(name)[:, (t - CT) * 16:(t - CT + 1) * 16].rearrange("p (a f) -> p a f", a=2)
                    return v.unsqueeze(1).to_broadcast([P, groups, 2, 8]) if groups > 1 else v
                cos, sin = tab("cos"), tab("sin")
                if groups > 1:
                    x = x.rearrange("p g (a s f) -> p g a s f", a=2, s=2)
                    x1, x2 = x[:, :, :, 0, :], x[:, :, :, 1, :]
                    n = groups * 16
                    t4 = [tmp[:, i * n:(i + 1) * n].rearrange("p (g a f) -> p g a f", g=groups, a=2) for i in range(4)]
                else:
                    x = x.rearrange("p (a s f) -> p a s f", a=2, s=2)
                    x1, x2 = x[:, :, 0, :], x[:, :, 1, :]
                    t4 = [tmp[:, i * 16:(i + 1) * 16].rearrange("p (a f) -> p a f", a=2) for i in range(4)]
                tt(t4[0], x1, cos, ALU.mult)
                tt(t4[1], x2, sin, ALU.mult)
                tt(t4[2], x2, cos, ALU.mult)
                tt(t4[3], x1, sin, ALU.mult)
                tt(x1, t4[0], t4[1], ALU.subtract)
                tt(x2, t4[2], t4[3], ALU.add)

            def attention(L, items, maps, p, PT, y, scale):
                def maxima(i, it):
                    ks = key_pieces(it[1])
                    for m in range(maps):
                        end = marks[("S", L, maps, it, m)]
                        dve.wait_ge(sems["a_done"], end)
                        for x, (off, n) in enumerate(ks):
                            b = ring_bank("a", end - len(ks) + x)
                            S(dve.tensor_reduce(s_mx[:, i % 2, m, x:x + 1], b[:, 0:n], AX.X, ALU.max))
                        if len(ks) == 2:
                            tt(s_mx[:, i % 2, m, 0:1], s_mx[:, i % 2, m, 0:1], s_mx[:, i % 2, m, 1:2], ALU.max)
                        ts(s_nb[:, i % 2, m:m + 1], s_mx[:, i % 2, m, 0:1], -scale, ALU.mult)
                        dve.sem_inc(sems["att_max"], 1)

                def sums(i, it, m):
                    r = s_rs[:, i % 2, m:m + 1]
                    if len(key_pieces(it[1])) == 2:
                        tt(r, s_sum[:, i % 2, m, 0:1], s_sum[:, i % 2, m, 1:2], ALU.add)
                    else:
                        copy(r, s_sum[:, i % 2, m, 0:1])
                    S(dve.reciprocal(r, r))

                def combine(i, it):
                    n = sum(n for _, n in key_pieces(it[1]))
                    dve.wait_ge(sems["att_p"], c.nth("att_p"))
                    for m in range(maps):
                        sums(i, it, m)
                    if maps == 2:
                        tt(s_rs[:, i % 2, 1:2], s_rs[:, i % 2, 1:2], s_lam[:, 4:5], ALU.mult)
                        ts(p(i % 2, 1)[:, 0:n], p(i % 2, 1)[:, 0:n], s_rs[:, i % 2, 1:2], ALU.mult)
                        stt(p(i % 2, 0)[:, 0:n], p(i % 2, 0)[:, 0:n], s_rs[:, i % 2, 0:1], p(i % 2, 1)[:, 0:n],
                            ALU.mult, ALU.subtract)
                        dve.sem_inc(sems["att_a"], 1)

                def turned(it):
                    n = sum(n for _, n in key_pieces(it[1]))
                    for at in range(0, n, 512):
                        ln = min(512, n - at)
                        dve.wait_ge(sems["d_done"], c.nth("d_done"))
                        b = bank()
                        copy(PT[:, at:at + ln], b[:, 0:ln])
                        dve.sem_inc(sems["d_free"], 1)

                def result(i, it):
                    dve.wait_ge(sems["d_done"], c.nth("d_done"))
                    b = bank()
                    o_ = y[:, it[1], it[0] * 64:it[0] * 64 + 64]
                    if maps == 1:
                        ts(o_, b[:, 0:64], s_rs[:, i % 2, 0:1], ALU.mult)
                    else:
                        copy(o_, b[:, 0:64])
                    dve.sem_inc(sems["d_free"], 1)

                maxima(0, items[0])
                combine(0, items[0])
                for i, it in enumerate(items):
                    if i + 1 < len(items):
                        maxima(i + 1, items[i + 1])
                    turned(it)
                    if i + 1 < len(items):
                        combine(i + 1, items[i + 1])
                    result(i, it)

            def head_norm(y, sc):
                t0 = QT[0]
                n = len(QT) * 4
                yv = y[:, t0:NT, :].rearrange("p t (h c) -> p (t h) c", h=4)
                sv = sc[:, 0:n * 64].rearrange("p (g c) -> p g c", c=64)
                tt(sv, yv, yv, ALU.mult)
                S(dve.tensor_reduce(s_hs[:, 0, 0:n], sv, AX.X, ALU.add))
                ts(s_hs[:, 1, 0:n], s_hs[:, 0, 0:n], 1.0 / 64, ALU.mult, EPS, ALU.add)
                if n < 24:
                    ts(s_hs[:, 1, n:24], s_hs[:, 1, n:24], 0.0, ALU.mult, 1.0, ALU.add)
                dve.sem_inc(sems["hs_ms"], 1)
                dve.wait_ge(sems["hs_rt"], c.nth("hs_rt"))
                S(dve.reciprocal(s_hs[:, 3, 0:n], s_hs[:, 2, 0:n]))
                tt(yv, yv, s_hs[:, 3, 0:n].unsqueeze(2).to_broadcast([P, n, 64]), ALU.mult)

            def finish(br, y, gain, factor=1.0):
                dve.sem_inc(sems["y_ready"], 1)
                for i in range(2):
                    for off, n in QS:
                        dve.wait_ge(sems["d_done"], c.nth("d_done"))
                        b = bank()
                        if gain is None:
                            copy(YT[:, br, i, off:off + n], b[:, 0:n])
                        else:
                            ts(YT[:, br, i, off:off + n], b[:, 0:n], gain[:, i:i + 1], ALU.mult, factor, ALU.mult)
                        dve.sem_inc(sems["d_free"], 1)
                dve.sem_inc(sems["branch_done"], 1)

            def mla(L):
                dve.wait_ge(sems["mla_lat"], c.nth("mla_lat"))
                q0 = QS[-1][0]
                tt(a_sq[:, 0:2, q0:T], a_ql[:, :, q0:T], a_ql[:, :, q0:T], ALU.mult)
                tt(a_sq[:, 2, :], a_kv, a_kv, ALU.mult)
                dve.sem_inc(sems["mla_sq"], 1)
                dve.wait_ge(sems["mla_r"], c.nth("mla_r"))
                S(dve.reciprocal(a_r[:, 0, q0:T], a_r[:, 0, q0:T]))
                S(dve.reciprocal(a_r[:, 1, :], a_r[:, 1, :]))
                for i in range(2):
                    stt(a_ql[:, i, q0:T], a_ql[:, i, q0:T], pk("g_q")[:, i:i + 1], a_r[:, 0, q0:T], ALU.mult, ALU.mult)
                stt(a_kv, a_kv, pk("g_kv"), a_r[:, 1, :], ALU.mult, ALU.mult)
                dve.sem_inc(sems["mla_n"], 1)
                dve.wait_ge(sems["mla_tm"], c.nth("mla_tm"))
                for t in range(CT, NT):
                    rope(a_qtm[:, t, :, 64:96], t, 4, a_tmp)
                    rope(a_kr[:, t, :], t, 1, a_tmp)
                for t in range(NT):
                    copy(a_ktm[:, t, :, 64:96], a_kr[:, t, :].unsqueeze(1).to_broadcast([P, 4, 32]))
                dve.sem_inc(sems["mla_rope"], 1)
                attention(L, [(h, t) for h in range(4) for t in QT], 1, lambda b, m: a_P[:, b, :], a_PT, a_y, 96 ** -0.5)
                ts(s_hs[:, 1, :], ones[:, 0:24], 1.0, ALU.mult)
                dve.sem_inc(sems["hs_ms"], 1)
                dve.wait_ge(sems["hs_rt"], c.nth("hs_rt"))
                finish(0, a_y, None)

            def mlstm(L):
                for at, w in ((0, 1), (257, 2), (771, 1)):
                    S(dve.memset(m_raw[:, :, at:at + w], 0.0))
                S(dve.memset(m_v[:, :, :, 64:65], 1.0))
                dve.wait_ge(sems["ml_raw"], c.nth("ml_raw"))
                wc = pk("w_conv").rearrange("p (i j) -> p i j", i=4)
                for i in range(4):
                    for off, n in (QS if i < 2 else SEG):
                        at = 0 if off == 0 else 258
                        tmp = m_tmp[:, 0:n]
                        ts(tmp, m_raw[:, i, at:at + n], wc[:, i, 0:1], ALU.mult, pk("b_conv")[:, i:i + 1], ALU.add)
                        stt(tmp, m_raw[:, i, at + 1:at + 1 + n], wc[:, i, 1:2], tmp, ALU.mult, ALU.add)
                        stt(m_qk[:, i, off:off + n], m_raw[:, i, at + 2:at + 2 + n], wc[:, i, 2:3], tmp, ALU.mult, ALU.add)
                dve.sem_inc(sems["ml_conv"], 1)
                ts(gF[0:8, :], gF[0:8, :], pk("b_f")[0:8, :], ALU.add)
                ts(gI[0:8, :], gI[0:8, :], pk("b_i")[0:8, :], ALU.add)
                dve.sem_inc(sems["ml_x"], 1)
                dve.wait_ge(sems["ml_l"], c.nth("ml_l"))
                ts(gF[0:8, :], gF[0:8, :], 0.0, ALU.min)
                tt(gF[0:8, :], gF[0:8, :], m_F[0:8, 0, :], ALU.subtract)
                one = ones[0:8, 0:1]
                for d in range(2):
                    F_, g_, M_ = m_F[0:8, d, :], m_g[0:8, d, :], m_M[0:8, d, :]

                    def runs(src):
                        if d == 0:
                            return [src[:, 0:T]]
                        return [src[:, CTX - 1::-1], src[:, T - 1:CTX - 1:-1]]

                    def last():
                        return 0
                    init = 0.0
                    for i, (f, x) in enumerate(zip(runs(F_), runs(gF[0:8, :]))):
                        scan(f, one.to_broadcast(list(x.shape)), x, 0.0 if i == 0 else F_[:, 0:1], ALU.mult, ALU.add)
                    tt(g_, gI[0:8, :], F_, ALU.subtract)
                    for i, (m, g) in enumerate(zip(runs(M_), runs(g_))):
                        scan(m, g, g, NEG_BIG if i == 0 else M_[:, 0:1], ALU.max, ALU.max)
                    tt(F_, F_, M_, ALU.add)
                dve.sem_inc(sems["ml_m"], 1)
                dve.wait_ge(sems["d_done"], c.nth("d_done"))
                b = bank()
                copy(m_gE, b[:, 0:192])
                dve.sem_inc(sems["d_free"], 1)
                dve.sem_inc(sems["ml_e"], 1)
                for h in range(4):
                    for j in range(NT):
                        qk = {}
                        for off, n in (QS if j < CT else QS[:1]):
                            dve.wait_ge(sems["d_done"], c.nth("d_done"))
                            qk[1 if off else 0] = bank()
                        dve.wait_ge(sems["ml_mask"], c.nth("ml_mask"))
                        for d in range(2):
                            tiles = ml_tiles(L, d, j)
                            for lat, (lo, hi) in enumerate(((0, CT), (CT, NT))):
                                r = [t for t in tiles if lo <= t < hi]
                                if r:
                                    a, z = r[0] * P, (r[-1] + 1) * P
                                    w = m_W[:, j % 2, d, a:z]
                                    stt(w, qk[lat][:, a - lo * P:z - lo * P], 0.125, w, ALU.mult, ALU.mult)
                        for _ in qk:
                            dve.sem_inc(sems["d_free"], 1)
                        dve.sem_inc(sems["ml_s"], 1)
                    dve.wait_ge(sems["pv_done"], (L * 4 + h + 1) * NT)
                    t0, nq = QT[0], len(QT)
                    for d in range(2):
                        acc = banks[6 + d][:, 0:NT * 65].rearrange("p (t c) -> p t c", t=NT)[:, t0:NT, :]
                        e = m_gE[:, 96 + d * 48:96 + d * 48 + 48].rearrange("p (t r) -> p t r", t=NT)[:, t0:NT, 4 * d + h]
                        copy(m_den[:, 1, 0:nq], acc[:, :, 64])
                        stt(m_den[:, 0, 0:nq], m_den[:, 1, 0:nq], -1.0, m_den[:, 1, 0:nq], ALU.mult, ALU.max)
                        tt(m_den[:, 0, 0:nq], m_den[:, 0, 0:nq], e, ALU.max)
                        S(dve.reciprocal(m_den[:, 1, 0:nq], m_den[:, 0, 0:nq]))
                        rb = m_den[:, 1, 0:nq].unsqueeze(2).to_broadcast([P, nq, 64])
                        yv = m_y[:, t0:NT, h * 64:h * 64 + 64]
                        if d == 0:
                            tt(yv, acc[:, :, 0:64], rb, ALU.mult)
                        else:
                            sc = m_sc[:, 0:nq * 64].rearrange("p (t c) -> p t c", t=nq)
                            tt(sc, acc[:, :, 0:64], rb, ALU.mult)
                            tt(yv, yv, sc, ALU.add)
                    dve.sem_inc(sems["x_free"], 1)
                head_norm(m_y, m_sc)
                gated(m_y, 1)
                finish(1, m_y, pk("g_ml"))

            def gated(y, br):
                for t in QT:
                    tt(y[:, t, :], y[:, t, :], YT[:, br, t // 3, (t % 3) * 256:(t % 3) * 256 + 256], ALU.mult)

            def gla(L):
                dve.wait_ge(sems["gl_in"], c.nth("gl_in"))
                dve.wait_ge(sems["gl_l"], c.nth("gl_l"))
                for d in range(2):
                    x = g_lg[:, d, :]
                    ts(x, x, 0.0, ALU.min)
                    tt(x, x, (g_t1, g_t2)[d], ALU.subtract)
                    ts(x, x, 1.0 / 16, ALU.mult)
                S(dve.memset(g_qm, 0.0))
                S(dve.memset(g_t2, 0.0))
                for d in range(2):
                    x = g_lg[:, d, :]
                    xs_ = x if d == 0 else x[:, ::-1]
                    o_ = g_t2 if d == 0 else g_t2[:, ::-1]
                    scan(o_, cc("resets"), xs_, 0.0, ALU.mult, ALU.add)
                    copy(x, g_t2)
                    xc = x.rearrange("p (c l) -> p c l", l=64)
                    end = xc[:, :, 63] if d == 0 else xc[:, :, 0]
                    copy(s_ge[:, d, :], end)
                    t1 = g_t1.rearrange("p (c l) -> p c l", l=64)
                    tt(t1, s_ge[:, d, :].unsqueeze(2).to_broadcast([P, 12, 64]), xc, ALU.subtract)
                    dve.sem_inc(sems["gl_g"], 1)
                    dve.wait_ge(sems["gl_e"], c.nth("gl_e"))
                    q0 = QS[-1][0]
                    tt(g_t1, g_t1, g_k, ALU.mult)
                    tt(g_ki, g_t2, g_k, ALU.mult)
                    stt(g_qd[:, q0:T], g_q[:, q0:T], 32 ** -0.5, g_lg[:, d, q0:T], ALU.mult, ALU.mult)
                    for h in range(4):
                        copy(g_qm[32 * h:32 * h + 32, h, q0:T], g_qd[32 * h:32 * h + 32, q0:T])
                    dve.sem_inc(sems["gl_ops"], 1)
                    for off, n in SEG:
                        dve.wait_ge(sems["d_done"], c.nth("d_done"))
                        b = bank()
                        copy(g_ke[:, off:off + n], b[:, 0:n])
                        dve.sem_inc(sems["d_free"], 1)
                    heads = cc("heads").unsqueeze(2).to_broadcast([P, 4, 64])
                    S(dve.memset(g_S[:, gla_chunk(d, 0), :], 0.0))
                    for i in range(11):
                        a, z = gla_chunk(d, i), gla_chunk(d, i + 1)
                        dve.wait_ge(sems["d_done"], c.nth("d_done"))
                        b = bank()
                        tt(g_sl.rearrange("p (h c) -> p h c", h=4), b[:, 0:256].rearrange("p (h c) -> p h c", h=4), heads, ALU.mult)
                        dve.sem_inc(sems["d_free"], 1)
                        stt(g_S[:, z, :], g_S[:, a, :], s_ge[:, d, a:a + 1], g_sl, ALU.mult, ALU.add)
                    dve.sem_inc(sems["gl_state"], 1)
                    mask = cc(("m_fwd", "m_bwd")[d]).unsqueeze(1).to_broadcast([P, 4, P])
                    for t in QT:
                        dve.wait_ge(sems["d_done"], c.nth("d_done"))
                        b = bank()
                        tt(g_A.rearrange("p (h c) -> p h c", h=4), b[:, :].rearrange("p (h c) -> p h c", h=4), mask, ALU.mult)
                        dve.sem_inc(sems["d_free"], 1)
                        dve.sem_inc(sems["gl_att"], 1)
                        dve.wait_ge(sems["d_done"], c.nth("d_done"))
                        b = bank()
                        if d == 0:
                            copy(g_y[:, t, :], b[:, 0:256])
                        else:
                            tt(g_y[:, t, :], b[:, 0:256], g_y[:, t, :], ALU.add)
                        dve.sem_inc(sems["d_free"], 1)
                head_norm(g_y, g_sc)
                gated(g_y, 2)
                finish(2, g_y, pk("g_gla"))

            def diff(L):
                lam0 = 0.8 - 0.6 * math.exp(-0.3 * L)
                lv = pk("lam")
                for i in range(2):
                    tt(s_l[:, 32 * i:32 * i + 32], lv[:, 64 * i:64 * i + 32], lv[:, 64 * i + 32:64 * i + 64], ALU.mult)
                    S(dve.tensor_reduce(s_lam[:, i:i + 1], s_l[:, 32 * i:32 * i + 32], AX.X, ALU.add))
                dve.sem_inc(sems["lam_p"], 1)
                dve.wait_ge(sems["lam_e"], c.nth("lam_e"))
                stt(s_lam[:, 4:5], s_lam[:, 2:3], lam0, s_lam[:, 3:4], ALU.add, ALU.subtract)
                dve.wait_ge(sems["mla_tm"], c.nth("mla_tm"))
                for t in range(CT, NT):
                    rope(d_tm[:, t, :].rearrange("p (g c) -> p g c", c=32), t, 16, d_tmp)
                dve.sem_inc(sems["mla_rope"], 1)
                attention(L, [(h, t) for h in range(4) for t in QT], 2, lambda b, m: d_P[:, b, m, :], d_PT, d_y, 32 ** -0.5)
                head_norm(d_y, d_sc)
                finish(3, d_y, pk("g_diff"), 1.0 - lam0)

            def merge(L):
                i = 0
                for half in range(2):
                    for n_ in range(4):
                        for d4 in range(4):
                            dt = half * 4 + d4
                            for off, ln in QS:
                                dve.wait_ge(sems["d_done"], c.nth("d_done"))
                                b = bank()
                                dve.wait_ge(sems["gate"], c.nth("gate"))
                                m = g_mT[:, dt, off:off + ln]
                                if n_ == 0:
                                    tt(m, g_gb[:, i % 2, 0:ln], b[:, 0:ln], ALU.mult)
                                else:
                                    pb = g_pb[:, i % 2, 0:ln]
                                    tt(pb, g_gb[:, i % 2, 0:ln], b[:, 0:ln], ALU.mult)
                                    tt(m, m, pb, ALU.add)
                                dve.sem_inc(sems["d_free"], 1)
                                dve.sem_inc(sems["mg_prod"], 1)
                                i += 1
                dve.sem_inc(sems["mg_sum"], 1)
                dve.wait_ge(sems["yo"], c.nth("yo"))
                t0 = QT[0]
                tt(s_ssq[:, t0:NT], s_ssq2[:, 0, t0:NT], s_ssq2[:, 1, t0:NT], ALU.add)
                ts(s_ms, s_ms, 0.0, ALU.mult, 1.0, ALU.add)
                ts(s_ms[:, t0:NT], s_ssq[:, t0:NT], 1.0 / D, ALU.mult, EPS, ALU.add)
                dve.sem_inc(sems["ms"], 1)
                dve.wait_ge(sems["rt"], c.nth("rt"))
                S(dve.reciprocal(s_r[:, t0:NT], s_rt[:, t0:NT]))
                residual(0, o_y, o_row, o_diag)

            def residual(s, y, row, diag):
                for i, (off, n) in enumerate(QS):
                    j = 0 if off else 1
                    for k in range(KD):
                        ts(diag[:, k, :], ident, s_G[:, s, j, k:k + 1], ALU.mult)
                    dve.sem_inc(sems["diag"], 1)
                    dve.wait_ge(sems["grow"], c.nth("grow"))
                    for t in range(off // P, (off + n) // P):
                        stt(y[:, t, :], y[:, t, :], s_r[:, t:t + 1], row, ALU.mult, ALU.mult)
                        tt(X[:, t, :], X[:, t, :], y[:, t, :], ALU.add)
                    if i + 1 < len(QS):
                        dve.sem_inc(sems["row_free"], 1)
                dve.sem_inc(sems["layer_done"], 1)

            def route(L):
                t0, nq = QT[0], len(QT)
                dve.wait_ge(sems["d_done"], c.nth("d_done"))
                b = bank()
                lg = b[:, t0 * NE:NT * NE].rearrange("p (t e) -> p t e", t=nq)
                S(dve.tensor_reduce(s_soft[:, 0, 0:nq], lg, AX.X, ALU.max))
                a = e_aff[:, t0:NT, :]
                tt(a, lg, s_soft[:, 0, 0:nq].unsqueeze(2).to_broadcast([P, nq, NE]), ALU.subtract)
                dve.sem_inc(sems["d_free"], 1)
                dve.sem_inc(sems["rt_max"], 1)
                dve.wait_ge(sems["rt_exp"], c.nth("rt_exp"))
                S(dve.tensor_reduce(s_soft[:, 0, 0:nq], a, AX.X, ALU.add))
                S(dve.reciprocal(s_soft[:, 1, 0:nq], s_soft[:, 0, 0:nq]))
                tt(a, a, s_soft[:, 1, 0:nq].unsqueeze(2).to_broadcast([P, nq, NE]), ALU.mult)
                dve.sem_inc(sems["aff"], 1)
                for off, n in QS:
                    dve.wait_ge(sems["d_done"], c.nth("d_done"))
                    b = bank()
                    copy(e_affT[0:NE, off:off + n], b[0:NE, 0:n])
                    dve.sem_inc(sems["d_free"], 1)
                for off, n in QS:
                    cap = CAP_L if off else CAP_C
                    v, wk, mk, cu = (x[0:NE, off:off + n] for x in (e_affT, e_wk, e_mk, e_cu))
                    copy(wk, v)
                    for r in range(cap // 8):
                        S(dve.max(s_top[0:NE, r, :], wk))
                        if r + 1 < cap // 8:
                            S(dve.match_replace(wk, s_top[0:NE, r, :], wk, -1.0))
                    low = s_top[0:NE, cap // 8 - 1, 7:8]
                    ts(mk, v, low, ALU.is_gt)
                    S(dve.tensor_reduce(s_cnt[0:NE, 0:1], mk, AX.X, ALU.add))
                    ts(s_cnt[0:NE, 1:2], s_cnt[0:NE, 0:1], -1.0, ALU.mult, float(cap), ALU.add)
                    ts(wk, v, low, ALU.is_equal)
                    one = ones[0:NE, 0:1].to_broadcast([NE, n])
                    scan(cu, one, wk, 0.0, ALU.mult, ALU.add)
                    stt(wk, cu, s_cnt[0:NE, 1:2], wk, ALU.is_le, ALU.mult)
                    tt(mk, mk, wk, ALU.add)
                    scan(cu, one, mk, 0.0, ALU.mult, ALU.add)
                    tt(mk, mk, cu, ALU.mult)
                dve.sem_inc(sems["pos"], 1)
                dve.wait_ge(sems["d_done"], c.nth("d_done"))
                b = bank()
                copy(e_pos[:, t0:NT, :], b[:, t0 * NE:NT * NE].rearrange("p (t e) -> p t e", t=nq))
                dve.sem_inc(sems["d_free"], 1)

            def moe(L):
                route(L)
                t0, nq = QT[0], len(QT)
                S(dve.memset(facc[:, t0:NT, :], 0.0))
                dve.sem_inc(sems["zeros"], 1)
                S(dve.memset(e_sel, 0.0))
                ts(e_ta[:, :, 0], cc("tokens"), -float(first_row[L]), ALU.add)
                cap = CAPS if len(QS) == 2 else CAP_L
                both = P if cap == 64 else cap

                def select(e):
                    copy(s_pc[:, 0, t0:NT], e_pos[:, t0:NT, bass.ds(e, 1)].squeeze(2))
                    copy(e_ta[:, t0:NT, 1], e_aff[:, t0:NT, bass.ds(e, 1)].squeeze(2))
                    for off, n in QS:
                        a, b = off // P, (off + n) // P
                        w0, cp = (0, CAP_L) if off else (CAP_L, CAP_C)
                        tt(e_sel[:, a:b, w0:w0 + cp], cc("iota")[:, 0:cp].unsqueeze(1).to_broadcast([P, b - a, cp]),
                           s_pc[:, 0, a:b].unsqueeze(2).to_broadcast([P, b - a, cp]), ALU.is_equal)
                    dve.sem_inc(sems["sel"], 1)

                def next_chosen():
                    dve.wait_ge(sems["chosen"], c.nth("chosen"))
                    copy(idx[0:cap, 0:1], banks[5][0:cap, 0:1])
                    copy(s_sel[0:both, 0:1], banks[5][0:both, 1:2])
                    dve.sem_inc(sems["idx_next"], 1)

                def now_chosen():
                    copy(idx[0:cap, 1:2], idx[0:cap, 0:1])
                    copy(s_sel[0:both, 1:2], s_sel[0:both, 0:1])
                    dve.sem_inc(sems["idx_now"], 1)

                def tokens():
                    dve.wait_ge(sems["rows_t"], c.nth("rows_t"))
                    for off, n in QS:
                        j, at, cp = (0, 0, CAP_L) if off else (1, CAP_L, CAP_C)
                        for q in range(2):
                            tt(e_xs[:, 4 * q:4 * q + 4, at:at + cp],
                               banks[2 + q][:, 0:4 * cap].rearrange("p (k j) -> p k j", k=4)[:, :, at:at + cp],
                               s_A[:, 1, j, 4 * q:4 * q + 4].unsqueeze(2).to_broadcast([P, 4, cp]), ALU.mult)
                        x = e_xs[:, :, at:at + cp]
                        tt(x, x, s_B[:, 1, j, :].unsqueeze(2).to_broadcast([P, KD, cp]), ALU.add)
                    dve.sem_inc(sems["xs"], 1)

                def hidden(g):
                    dve.wait_ge(sems["silu"], c.nth("silu"))
                    dve.wait_ge(sems["gu"], c.nth("gu", 2))
                    n = EXP_W[2 * g]
                    for rows, c0, c1 in parts(n, cap):
                        tt(e_hid[0:rows, 512 * g + c0:512 * g + c1], e_sg[0:rows, g % 2, c0:c1],
                           banks[(0, 2, 0)[g] + 1][0:rows, c0:c1], ALU.mult)
                    dve.sem_inc(sems["hid"], 1)

                def expert(e, last):
                    if not last:
                        select(e + 1)
                    hidden(0)
                    if not last:
                        next_chosen()
                    hidden(1)
                    hidden(2)
                    if not last:
                        tokens()
                    dve.wait_ge(sems["ys"], c.nth("ys", 3))
                    ts(e_ys[0:cap, 512:1024], banks[7][both - cap:both, :], s_sel[both - cap:both, 1:2], ALU.mult)
                    dve.sem_inc(sems["ys_d"], 1)
                    if not last:
                        dve.wait_ge(sems["scat"], c.nth("scat", 16))
                        now_chosen()

                select(0)
                next_chosen()
                tokens()
                now_chosen()
                dve.sem_inc(sems["ys_d"], 1)
                per = {"silu": 3, "gu": 6, "chosen": 1, "rows_t": 1, "ys": 3, "scat": 16,
                       "dve_order": 2 + len(QS) + 2 + 3 + (cap == 64) + 3 * len(QS) + 1 + 2}
                with dve.Fori(0, NE - 1) as e:
                    c.begin(e, per)
                    expert(e, False)
                    c.e = None
                c.finish_loop(NE - 1)
                expert(NE - 1, True)
                c.nth("scat", 16)
                norm_apply(None, QT, None)
                residual(1, facc, e_row, o_diag)

            dve.wait_ge(sems["const_in"], 16)
            dve.wait_ge(sems["x_in"], 48)
            S(dve.memset(s_hs, 1.0))
            S(dve.memset(s_ms, 1.0))
            for L in range(DEPTH):
                SEG, QS, QT = segs(L), segs(L, True), qtiles(L)
                dve.wait_ge(sems["pack_in"], 16 * (2 * L + 1))
                modulation(L)
                norm_apply(V_N["xn"].rearrange("p (t d) -> p t d", t=NT), list(range(NT)), X)
                mla(L)
                mlstm(L)
                gla(L)
                diff(L)
                merge(L)
                norm_apply(e_xn, QT, X)
                moe(L)
                SEG = QS

        @block.gpsimd
        def _(pool):
            c = Order(pool, sems, "pool_order")

            def moe(L):
                t0 = qtiles(L)[0]
                cap = CAP_L if t0 else CAPS
                tiles = lambda a: a.rearrange("(t p) d -> p t d", p=P)
                pool.wait_ge(sems["xn"], 2 * L + 2)
                pool.dma_start(tiles(xn_rows[L]), e_xn[:, t0:NT, :]).then_inc(sems["xn_stored"], 16)
                pool.wait_ge(sems["zeros"], c.nth("zeros"))
                pool.dma_start(tiles(f_rows[L]), facc[:, t0:NT, :]).then_inc(sems["zeroed"], 16)
                pool.wait_ge(sems["xn_stored"], c.nth("xn_stored", 16))
                pool.wait_ge(sems["zeroed"], c.nth("zeroed", 16))

                def gather():
                    pool.wait_ge(sems["idx_next"], c.nth("idx_next"))
                    pool.nop(nofuse=True)
                    pool.indirect_dma_start(e_rows[0:cap, :], None, xn_rows[L][:, :],
                                            bass.IndirectOffsetOnAxis(idx[0:cap, 0:1], 0)).then_inc(sems["rows_in"], 16)

                def scatter():
                    pool.wait_ge(sems["idx_now"], c.nth("idx_now"))
                    pool.wait_ge(sems["ys_a"], c.nth("ys_a"))
                    pool.wait_ge(sems["ys_d"], c.nth("ys_d"))
                    pool.nop(nofuse=True)
                    pool.indirect_dma_start(f_rows[L][:, :], bass.IndirectOffsetOnAxis(idx[0:cap, 1:2], 0), e_ys[0:cap, :], None,
                                            compute_op=ALU.add).then_inc(sems["scat"], 16)
                    pool.wait_ge(sems["scat"], c.nth("scat", 16))

                gather()
                c.nth("ys_a")
                c.nth("ys_d")
                per = {"idx_next": 1, "rows_t": 1, "idx_now": 1, "ys_a": 1, "ys_d": 1, "scat": 16}
                with pool.Fori(0, NE - 1) as e:
                    c.begin(e, per)
                    pool.wait_ge(sems["rows_t"], c.nth("rows_t"))
                    gather()
                    scatter()
                    c.e = None
                c.finish_loop(NE - 1)
                scatter()
                c.nth("rows_t")
                pool.dma_start(facc[:, t0:NT, :], tiles(f_rows[L])).then_inc(sems["f_back"], 16)

            for L in range(DEPTH):
                for h in range(4):
                    for j in range(NT):
                        pool.wait_ge(sems["ml_w"], c.nth("ml_w"))
                        for d in range(2):
                            if j not in ml_tiles(L, d, j):
                                continue
                            w = m_W[:, j % 2, d, j * P:(j + 1) * P]
                            sgn = 1 if d == 0 else -1
                            c.seq(pool.affine_select(out=w, in_=w, pattern=[[sgn, P]], compare_op=ALU.is_ge, fill=0.0,
                                                     base=0, channel_multiplier=-sgn))
                        pool.sem_inc(sems["ml_mask"], 1)
                moe(L)

        def need(eng, n):
            if n in piece_done:
                name, v = piece_done[n]
                eng.wait_ge(sems[name], v)
            else:
                L = max(L for L in range(DEPTH) if N_EXP[L] <= n)
                i = n - (N_IN[L + 1] - SLOTS)
                assert 0 <= i < SLOTS
                eng.wait_ge(sems["ys"], (L + 1) * NE * 3 - (SLOTS - 1 - i))

        @block.sync
        def _(sp):
            sp.dma_start(const[:, :], I["const"]).then_inc(sems["const_in"], 16)
            sp.dma_start(packs[:, :], I["pack"][0]).then_inc(sems["pack_in"], 16)
            sp.dma_start(s_cs, I["cs"].rearrange("p (k j) -> p k j", k=KD)).then_inc(sems["x_in"], 16)
            sp.dma_start(X[:, CT:NT, :], I["x"][0].rearrange("(t p) d -> p t d", p=P)).then_inc(sems["x_in"], 16)
            sp.dma_start(X[:, 0:CT, :], I["ctx"][0].rearrange("(t p) d -> p t d", p=P)).then_inc(sems["x_in"], 16)
            def stream(n, w, kk, src):
                if n >= SLOTS:
                    need(sp, n - SLOTS)
                sp.dma_start(slot(n, w, kk), src).then_inc(sems[f"w_in{n % SLOTS}"], 16)

            for i, (w, kk, src) in enumerate(ada_pieces(0)):
                stream(N_ADA[0] + i, w, kk, src)
            for L in range(DEPTH):
                if L:
                    sp.wait_ge(sems["layer_done"], 2 * L)
                    sp.dma_start(packs[:, :], I["pack"][L]).then_inc(sems["pack_in"], 16)
                for i, (w, kk, src) in enumerate(in_pieces(L)):
                    stream(N_IN[L] + i, w, kk, src)
                if L + 1 < DEPTH:
                    for i, (w, kk, src) in enumerate(ada_pieces(L + 1)):
                        stream(N_ADA[L + 1] + i, w, kk, src)
                sp.wait_ge(sems["branch_done"], 4 * (L + 1))
                sp.dma_start(g_wbr, I["w_branch"][L].rearrange("b (i p) n -> p (b i) n", p=P)).then_inc(sems["pack_in"], 16)
                for i, (w, kk, src) in enumerate(merge_pieces(L)):
                    stream(N_MERGE[L] + i, w, kk, src)
                n0 = N_EXP[L]

                def piece(e, i):
                    if i < 6:
                        s = (i // 2) * 512
                        src = I[("w_e_gate", "w_e_up")[i % 2]][L, e, :, s:s + EXP_W[i]].rearrange("(k p) n -> p k n", p=P)
                        sp.dma_start(slot(n0 + i, EXP_W[i]), src).then_inc(sems[f"w_in{(n0 + i) % SLOTS}"], 16)
                    else:
                        r = (i - 6) * 512
                        kk = EXP_DOWN[i - 6]
                        src = I["w_e_down"][L, e, r:r + kk * P, :].rearrange("(k p) n -> p k n", p=P)
                        sp.dma_start(slot(n0 + i, 1024, kk), src).then_inc(sems[f"w_in{(n0 + i) % SLOTS}"], 16)

                def freed(e, i):
                    i -= SLOTS
                    if i < 0:
                        i, e = i + PIECES_EXP, e - 1
                    if i < 6:
                        sp.wait_ge(sems["gu"], e * 6 + (L * NE * 6 + i + 1))
                    else:
                        sp.wait_ge(sems["ys"], e * 3 + (L * NE * 3 + i - 6 + 1))

                for i in range(PIECES_EXP):
                    if i < SLOTS:
                        need(sp, n0 + i - SLOTS)
                    else:
                        freed(0, i)
                    piece(0, i)
                with sp.Fori(1, NE) as e:
                    for i in range(PIECES_EXP):
                        freed(e, i)
                        piece(e, i)
            sp.wait_ge(sems["layer_done"], 2 * DEPTH)
            sp.dma_start(out[0].rearrange("(t p) d -> p t d", p=P), X[:, CT:NT, :]).then_inc(sems["out_done"], 16)
            sp.wait_ge(sems["out_done"], 16)


def key_pieces(t):
    return [(0, CTX)] if t < CT else [(0, 512), (512, T - 512)]


def ml_tiles(L, d, j):
    first = CT if L == DEPTH - 1 else 0
    if d == 0:
        ts = range(j, NT)
    elif j < CT:
        ts = list(range(0, j + 1)) + list(range(CT, NT))
    else:
        ts = range(CT, j + 1)
    return [t for t in ts if t >= first]


def ml_last(d, t):
    if d == 0:
        return t
    return CT - 1 if t < CT else NT - 1


def gla_chunk(d, i):
    nc_ = CTX // 64
    if d == 0:
        return i
    return nc_ - 1 - i if i < nc_ else T // 64 - 1 - (i - nc_)


def _cols(a, n):
    return np.asarray(a).reshape(n, P).T


def pack_layer(I, L):
    p = np.zeros((P, PACK_W), np.float32)

    def put(name, a):
        s, w = PK[name]
        p[:a.shape[0], s:s + w] = a

    for n in ("g_mix_pre", "g_ffn_pre", "g_mix_post", "g_ffn_post"):
        put(n, _cols(I[n][L], 8))
    put("b_ada", _cols(I["b_ada"][L], 48))
    put("g_q", _cols(I["g_q_lat"][L], 2))
    put("g_kv", _cols(I["g_kv_lat"][L], 1))
    put("w_conv", I["w_conv"][L].reshape(3, 4, P).transpose(2, 1, 0).reshape(P, 12))
    put("b_conv", _cols(I["b_conv"][L], 4))
    put("b_alpha", _cols(I["b_alpha"][L], 2))
    put("g_ml", _cols(I["g_mlstm_out"][L], 2))
    put("g_gla", _cols(I["g_gla_out"][L], 2))
    put("g_diff", _cols(I["g_diff_out"][L], 2))
    put("b_gate", _cols(I["b_gate"][L], 32))
    put("w_router", I["w_router"][L].reshape(8, P, NE).transpose(1, 0, 2).reshape(P, 128))
    put("lam", np.broadcast_to(I["diff_lambda"][L].reshape(1, 128), (P, 128)))
    put("b_i", I["b_igate"][L].reshape(8, 1))
    put("b_f", I["b_fgate"][L].reshape(8, 1))
    put("w_alpha", I["w_alpha2"][L].transpose(1, 0, 2).reshape(16, 256))
    put("w_uq", I["w_uq"][L].reshape(2, P, 384).transpose(1, 0, 2).reshape(P, 768))
    put("w_ukv", I["w_ukv"][L])
    return p


def order_w_in(w):
    L = w.shape[0]
    z = np.zeros((L, D, sum(W_IN_SPLIT)), w.dtype)
    ml, gl, df = 416, 1456, 2256
    z[:, :, 0:416] = w[:, :, 0:416]
    z[:, :, 416:424] = w[:, :, ml + 1024:ml + 1032]
    z[:, :, 448:456] = w[:, :, ml + 1032:ml + 1040]
    z[:, :, 456:1480] = w[:, :, ml:ml + 1024]
    z[:, :, 1480:1496] = w[:, :, gl + 768:gl + 784]
    z[:, :, 1512:1528] = w[:, :, gl + 784:gl + 800]
    z[:, :, 1528:1784] = w[:, :, gl:gl + 256]
    z[:, :, 1784:2296] = w[:, :, gl + 256:gl + 768]
    z[:, :, 2296:3064] = w[:, :, df:df + 768]
    return z


def kernel(**inputs):
    import concourse.bacc as bacc
    from concourse.bass_utils import run_bass_kernel_spmd as run

    I = {k: np.ascontiguousarray(v) for k, v in inputs.items()}
    cs = np.stack([_cols(I["c"][0], 8), _cols(I["c_ctx"], 8)], -1).reshape(P, 16)
    arrays = {
        "x": I["x"], "ctx": I["ctx"], "cs": np.ascontiguousarray(cs), "const": constants(),
        "pack": np.stack([pack_layer(I, L) for L in range(DEPTH)]), "w_in": order_w_in(I["w_in"]),
    }
    for n in ("w_ada", "w_branch", "w_gate", "w_out", "w_e_gate", "w_e_up", "w_e_down"):
        arrays[n] = I[n]
    nc = bacc.Bacc("TRN2", target_bir_lowering=False, num_devices=1)
    aps = {n: nc.dram_tensor(f"in_{n}", a.shape, F32, kind="ExternalInput").ap() for n, a in arrays.items()}
    out = nc.dram_tensor("out_x", (1, LAT, D), F32, kind="ExternalOutput").ap()
    hybrid_layers(nc, aps, out)
    r = run(nc, [{f"in_{n}": a for n, a in arrays.items()}], core_ids=[0])
    return r.results[0]["out_x"]
```
